# Optimizing a Trainium2 kernel written in Bass

```python
import jax, jax.numpy as jnp
from jax import lax
import numpy as np

D_MODEL = 1024
BATCH = 1
SEQ = 512
DEPTH = 1

MIX_WIDTH = D_MODEL
CONV_WIDTH = MIX_WIDTH // 2
ATTN_WIDTH = MIX_WIDTH - CONV_WIDTH
HEAD_DIM = 64
N_HEADS = ATTN_WIDTH // HEAD_DIM
CONV_K = 3
DILATED_PATTERNS = ((128, 1), (512, 4), (2048, 16))
ROPE_THETA = 500000.0
ROT_DIM = HEAD_DIM // 4
N_EXPERTS = 16
CAPACITY_FACTOR = 2
D_FF_EXPERT = 2 * D_MODEL
PROJ_WIDTH = 3 * CONV_WIDTH + 3 * ATTN_WIDTH
RMS_EPS = 1e-6
NEG_INF = -1e30

kernel_name = "hybrid_conv_dilated_attn_ec_moe_encoder"

def rmsnorm(x, g):
    xf = x.astype(jnp.float32)
    y = xf * lax.rsqrt(jnp.mean(xf * xf, axis=-1, keepdims=True) + RMS_EPS)
    return (y * g.astype(jnp.float32)).astype(x.dtype)

def partial_rope(t, positions):
    half = ROT_DIM // 2
    inv_freq = ROPE_THETA ** (-jnp.arange(half, dtype=jnp.float32) / half)
    ang = positions.astype(jnp.float32)[..., None] * inv_freq
    cos = jnp.cos(ang)[:, :, None, :]
    sin = jnp.sin(ang)[:, :, None, :]
    tf = t.astype(jnp.float32)
    t1, t2, rest = tf[..., :half], tf[..., half:ROT_DIM], tf[..., ROT_DIM:]
    out = jnp.concatenate([t1 * cos - t2 * sin, t2 * cos + t1 * sin, rest], axis=-1)
    return out.astype(t.dtype)

def centred_depthwise_conv(u, w):
    s = u.shape[1]
    up = jnp.pad(u, ((0, 0), (1, 1), (0, 0)))
    return w[0] * up[:, 0:s] + w[1] * up[:, 1:s + 1] + w[2] * up[:, 2:s + 2]

def dilated_band_attention(q, k, v, window, dil):
    b, s, h, dh = q.shape
    half = (window // 2) // dil
    blk = half
    L = s // dil
    nb = -(-L // blk)
    lp = nb * blk

    def to_sub(t):
        return t.reshape(b, L, dil, h, dh).transpose(0, 2, 3, 1, 4)

    qs = jnp.pad(to_sub(q), ((0, 0), (0, 0), (0, 0), (0, lp - L), (0, 0)))
    qs = qs.reshape(b, dil, h, nb, blk, dh)

    def key_blocks(t):
        tp = jnp.pad(to_sub(t), ((0, 0), (0, 0), (0, 0), (blk, lp - L + blk), (0, 0)))
        tp = tp.reshape(b, dil, h, nb + 2, blk, dh)
        return jnp.concatenate([tp[:, :, :, :nb], tp[:, :, :, 1:nb + 1], tp[:, :, :, 2:]], axis=-2)

    kb, vb = key_blocks(k), key_blocks(v)
    qpos = np.arange(nb)[:, None, None] * blk + np.arange(blk)[None, :, None]
    kpos = (np.arange(nb)[:, None, None] - 1) * blk + np.arange(3 * blk)[None, None, :]
    mask = (np.abs(qpos - kpos) <= half) & (kpos >= 0) & (kpos < L)

    sc = jnp.einsum('brhnqc,brhnkc->brhnqk', qs.astype(jnp.float32), kb.astype(jnp.float32))
    sc = jnp.where(mask, sc, NEG_INF)
    m = jnp.max(sc, axis=-1)
    p = jnp.where(mask, jnp.exp(sc - m[..., None]), 0.0)
    l = jnp.sum(p, axis=-1)
    num = jnp.einsum('brhnqk,brhnkc->brhnqc', p, vb.astype(jnp.float32))

    def from_sub(t):
        t = t.reshape((b, dil, h, lp) + t.shape[5:])[:, :, :, :L]
        t = jnp.moveaxis(t, 3, 1)
        return t.reshape((b, s, h) + t.shape[4:])

    return from_sub(num), from_sub(m), from_sub(l)

def mixed_dilated_attention(q, k, v):
    nums, ms, ls = [], [], []
    for window, dil in DILATED_PATTERNS:
        n_, m_, l_ = dilated_band_attention(q, k, v, window, dil)
        nums.append(n_); ms.append(m_); ls.append(l_)
    m_all = jnp.stack(ms)
    a = jnp.exp(m_all - jnp.max(m_all, axis=0, keepdims=True))
    den = jnp.sum(a * jnp.stack(ls), axis=0)
    num = jnp.sum(a[..., None] * jnp.stack(nums), axis=0)
    return (num / den[..., None]).astype(q.dtype)

def expert_choice_ffn(h, w_router, w_gate, w_up, w_down):
    b, s, d = h.shape
    cap = CAPACITY_FACTOR * s // N_EXPERTS
    logits = jnp.einsum('bsd,de->bse', h.astype(jnp.float32), w_router.astype(jnp.float32))
    aff = jax.nn.softmax(logits, axis=-1)
    gates, idx = lax.top_k(jnp.swapaxes(aff, 1, 2), cap)
    bidx = jnp.arange(b)[:, None, None]
    xe = h[bidx, idx]
    a = jnp.einsum('becd,edf->becf', xe, w_gate)
    u = jnp.einsum('becd,edf->becf', xe, w_up)
    y = jnp.einsum('becf,efd->becd', jax.nn.silu(a) * u, w_down)
    y = y * gates[..., None].astype(y.dtype)
    return jnp.zeros_like(h).at[bidx, idx].add(y)

def setup_inputs(seed: int = 0) -> dict:
    key = jax.random.key(seed)
    ks = jax.random.split(key, 16)
    f32 = jnp.float32
    nrm = lambda k, shape, fan: jax.random.normal(k, shape, f32) * (fan ** -0.5)
    gain = lambda k, shape: 1.0 + 0.02 * jax.random.normal(k, shape, f32)
    x = jax.random.normal(ks[0], (BATCH, SEQ, D_MODEL), f32)
    offsets = jax.random.randint(ks[1], (BATCH, 1), 0, 4096, dtype=jnp.int32)
    positions = offsets + jnp.arange(SEQ, dtype=jnp.int32)[None, :]
    return {
        "x": x,
        "positions": positions,
        "g_mix": gain(ks[2], (DEPTH, D_MODEL)),
        "w_in": nrm(ks[3], (DEPTH, D_MODEL, PROJ_WIDTH), D_MODEL),
        "conv_w": nrm(ks[4], (DEPTH, CONV_K, CONV_WIDTH), CONV_K),
        "g_conv_out": gain(ks[5], (DEPTH, CONV_WIDTH)),
        "g_attn_out": gain(ks[6], (DEPTH, ATTN_WIDTH)),
        "w_out": nrm(ks[7], (DEPTH, MIX_WIDTH, D_MODEL), MIX_WIDTH),
        "g_ffn": gain(ks[8], (DEPTH, D_MODEL)),
        "w_router": nrm(ks[9], (DEPTH, D_MODEL, N_EXPERTS), D_MODEL),
        "w_gate": nrm(ks[10], (DEPTH, N_EXPERTS, D_MODEL, D_FF_EXPERT), D_MODEL),
        "w_up": nrm(ks[11], (DEPTH, N_EXPERTS, D_MODEL, D_FF_EXPERT), D_MODEL),
        "w_down": nrm(ks[12], (DEPTH, N_EXPERTS, D_FF_EXPERT, D_MODEL), D_FF_EXPERT),
        "g_final": gain(ks[13], (D_MODEL,)),
    }

def reference(x, positions, g_mix, w_in, conv_w, g_conv_out, g_attn_out, w_out,
              g_ffn, w_router, w_gate, w_up, w_down, g_final):
    b, s, _ = x.shape
    splits = np.cumsum([CONV_WIDTH] * 3 + [ATTN_WIDTH] * 2).tolist()
    for layer in range(DEPTH):
        h = rmsnorm(x, g_mix[layer])
        p = jnp.einsum('bsd,dp->bsp', h, w_in[layer])
        c_b, c_c, c_u, q, k, v = jnp.split(p, splits, axis=-1)
        y_conv = c_b * centred_depthwise_conv(c_c * c_u, conv_w[layer])
        q = partial_rope(q.reshape(b, s, N_HEADS, HEAD_DIM), positions) * (HEAD_DIM ** -0.5)
        k = partial_rope(k.reshape(b, s, N_HEADS, HEAD_DIM), positions)
        v = v.reshape(b, s, N_HEADS, HEAD_DIM)
        y_attn = mixed_dilated_attention(q, k, v).reshape(b, s, ATTN_WIDTH)
        y = jnp.concatenate([rmsnorm(y_conv, g_conv_out[layer]),
                             rmsnorm(y_attn, g_attn_out[layer])], axis=-1)
        x = x + jnp.einsum('bsm,md->bsd', y, w_out[layer])
        h2 = rmsnorm(x, g_ffn[layer])
        x = x + expert_choice_ffn(h2, w_router[layer], w_gate[layer], w_up[layer], w_down[layer])
    return rmsnorm(x, g_final)


_drawn_inputs = setup_inputs


def setup_inputs(seed=0):
    import zlib

    import numpy as np

    out = dict(_drawn_inputs(seed))
    spreads = {}
    factors = {'g_conv_out': 4.672, 'g_attn_out': 4.27, 'g_ffn': 5.523, 'g_final': 2.746}
    for name, (base, spread) in spreads.items():
        noise = np.random.default_rng([zlib.crc32(name.encode()), seed]).standard_normal(out[name].shape)
        drawn = base * np.exp(spread * noise) if base else spread * noise
        out[name] = __import__('jax').numpy.asarray(drawn.astype(out[name].dtype))
    for name, factor in factors.items():
        out[name] = (out[name] * factor).astype(out[name].dtype)
    return out
```

```python
import math
from contextlib import ExitStack

import numpy as np

import concourse.bass as bass
from concourse import mybir

P = 128
F32 = mybir.dt.float32
I32 = mybir.dt.int32
ALU = mybir.AluOpType
ACT = mybir.ActivationFunctionType
AX = mybir.AxisListType

HEAD_DIM = 64
ROT_HALF = HEAD_DIM // 8
ROPE_THETA = 500000.0
RMS_EPS = 1e-6
MASKED = -1e30
CAPACITY_FACTOR = 2
PATTERNS = ((128, 1), (512, 4), (2048, 16))

def turn_parts(bits, count):
    left, parts = 2.0 * math.pi, []
    for _ in range(count):
        unit = 2.0 ** (math.floor(math.log2(left)) + 1 - bits)
        parts.append(math.floor(left / unit) * unit)
        left -= parts[-1]
    return (*parts, left)


TURN_PARTS = turn_parts(10, 3)
ROUND = 12582912.0
PI_INSIDE = 3.1415925


def hybrid_layer(nc, x_d, positions_d, g_mix_d, w_in_d, conv_w_d, g_conv_d, g_attn_d, w_out_d,
                 g_ffn_d, w_router_d, w_gate_d, w_up_d, w_down_d, g_final_d, out_d):
    _, S, D = x_d.shape
    _, E, _, F = w_gate_d.shape
    W = D // 2
    NT = S // P
    KD = D // P
    KW = W // P
    NH = W // HEAD_DIM
    CAP = CAPACITY_FACTOR * S // E
    B = 512
    ROUNDS = F // (2 * B)
    PAIRS = E // 2
    TAPS = conv_w_d.shape[1]
    assert S == B and D == 2 * B and CAP == 64 and NH == 2 * KW and TAPS == 3

    RING = 16
    SLOT = 2048
    FRONT_SLOTS = 16
    ROUND_SLOTS = 2 * (D // 256)
    EXPERT_SLOTS = ROUNDS * ROUND_SLOTS + F // 256
    PAIR_SLOTS = 2 * EXPERT_SLOTS
    assert PAIR_SLOTS % RING == 0 and FRONT_SLOTS == RING
    W_IN_COLUMNS = (W, 2 * W, 0, W + 256, 2 * W + 256, 256,
                    5 * W, 5 * W + 256, 3 * W, 3 * W + 256, 4 * W, 4 * W + 256)
    UNITS = KW * NT

    with ExitStack() as es:
        def sb(name, shape, dt=F32):
            return es.enter_context(nc.sbuf_tensor(name, shape, dt))

        def sem(name):
            return es.enter_context(nc.semaphore(name))

        ring = sb("ring", [P, RING, SLOT])
        x_reg = sb("x_reg", [P, NT * D])
        x_sb = x_reg[:, :].rearrange("p (t d) -> p t d", t=NT)
        qk_stage = [x_reg[:, 1024 * b:1024 * b + 1024] for b in range(2)]
        conv_sq, conv_sq1 = x_reg[:, 2048:2560], x_reg[:, 2560:3072]
        rot = x_reg[:, 3072:3584].rearrange("p (i h c) -> p i h c", i=4, h=2 * NH)
        scores = [x_reg[:, 1024 * b:1024 * b + 1024].rearrange("p (h k) -> p h k", h=2) for b in range(4)]
        r1 = sb("r1", [P, 4096])
        hT = r1[:, :].rearrange("p (k t) -> p k t", k=KD)
        yT_attn = r1[:, 0:2048].rearrange("p (m t) -> p m t", m=KW)
        probT = [r1[:, 2048 + 1024 * b:3072 + 1024 * b] for b in range(2)]
        h2T = [r1[:, 2048 + 1024 * b:3072 + 1024 * b] for b in range(2)]
        xeT = r1[:, 0:1024].rearrange("p (k s) -> p k s", k=KD)
        hidT = r1[:, 1024:2048].rearrange("p (f s) -> p f s", s=CAP)
        r2 = sb("r2", [P, 6144])
        xn = r2[:, 0:4096].rearrange("p (t d) -> p t d", t=NT)
        qT = r2[:, 0:2048].rearrange("p (m t) -> p m t", m=KW)
        kT = r2[:, 2048:6144].rearrange("p (h m t) -> p h m t", h=2, m=KW)
        attn_sq, attn_sq1 = r2[:, 0:512], r2[:, 512:1024]
        h2 = xn
        g_ffn, g_final = r2[:, 4096:5120], r2[:, 5120:6144]
        dist, mask_a, mask_b = r2[:, 4096:4992], r2[:, 4992:5888], x_reg[:, 3072:3968]
        ZW = S + 2
        r3 = sb("r3", [P, 2 * ZW + 2 * S])
        z_buf = [r3[:, ZW * b:ZW * b + ZW] for b in range(2)]
        c_buf = [r3[:, 2 * ZW + S * b:2 * ZW + S * b + S] for b in range(2)]
        v_sb = r3[:, 0:2048].rearrange("p (t c) -> p t c", t=NT)
        top_row = [r3[0:E, 512 * b:512 * b + 512] for b in range(3)]
        silu = [r3[:, 512 * b:512 * b + 512] for b in range(2)]
        hid = [r3[:, 1024 + 512 * b:1536 + 512 * b] for b in range(2)]
        r4 = sb("r4", [P, 2048])
        g_mix = r4[:, 0:1024]
        gain_rows = r4[0:20, 1024:1152]
        pos_int, pos_rows = r4[0:NT, 1152:1280], r4[0:NT, 1280:1408]
        yT_conv = r4[:, :].rearrange("p (m t) -> p m t", m=KW)
        y_pair = r4[:, 0:1024]
        gated = r4[:, 1024:1536].rearrange("p (t j s) -> p t j s", t=NT, j=2)
        putT = r4[:, 1536:2048]
        strip = sb("strip", [P, 2 * S - P])
        picks = strip[:, 0:512].rearrange("p (t j s) -> p t j s", t=NT, j=2)
        ident = sb("ident", [P, P])
        ones = sb("ones", [P, 1])
        slot_ids = sb("slot_ids", [P, CAP])
        router = sb("router", [P, KD * E])
        inv_freq = sb("inv_freq", [P, ROT_HALF])
        angles = sb("angles", [P, NT * ROT_HALF])
        turns = sb("turns", [P, 2 * NT * ROT_HALF])
        reduced = sb("reduced", [P, 2 * NT * ROT_HALF])
        sin_cos = sb("sin_cos", [P, 2 * NT * ROT_HALF])
        columns = sb("columns", [P, 24])
        sums = sb("sums", [P, 3 * NT])
        norm = sb("norm", [P, 14, 4, NT])
        row_max = sb("row_max", [P, 2 * UNITS])
        neg_max = sb("neg_max", [P, 2 * UNITS])
        row_sum = sb("row_sum", [P, 2 * UNITS])
        row_inv = sb("row_inv", [P, 2 * UNITS])
        aff = sb("aff", [P, NT, E])
        slot_of = sb("slot_of", [P, NT, E])
        small = sb("small", [P, 3, NT])
        top8 = sb("top8", [E, 8])
        bank = es.enter_context(nc.psum_tensor("bank", [P, 8, B], F32))

        x_loaded = [sem(f"x_loaded{t}") for t in range(NT)]
        g_mix_loaded = sem("g_mix_loaded")
        rows_loaded = sem("rows_loaded")
        router_loaded = sem("router_loaded")
        x_reloaded = sem("x_reloaded")
        gains_loaded = sem("gains_loaded")
        slot_loaded = [sem(f"slot_loaded{s}") for s in range(RING)]
        slots_used = sem("slots_used")
        out_stored = sem("out_stored")
        pool_step = sem("pool_step")
        consts_ready = sem("consts_ready")
        pos_ready = sem("pos_ready")
        rows_turned = sem("rows_turned")
        columns_ready = sem("columns_ready")
        dve_step = sem("dve_step")
        squared = sem("squared")
        var_ready = sem("var_ready")
        root_ready = sem("root_ready")
        xn_ready = sem("xn_ready")
        xn_turned = sem("xn_turned")
        hT_ready = sem("hT_ready")
        strip_ready = sem("strip_ready")
        turns_ready = sem("turns_ready")
        sin_ready = sem("sin_ready")
        kT_zeroed = sem("kT_zeroed")
        conv_done = sem("conv_done")
        c_copied = sem("c_copied")
        y_conv_ready = sem("y_conv_ready")
        conv_sq_ready = sem("conv_sq_ready")
        conv_sums_done = sem("conv_sums_done")
        y_conv_scaled = sem("y_conv_scaled")
        qkv_done = sem("qkv_done")
        v_copied = sem("v_copied")
        qk_copied = sem("qk_copied")
        rope_done = sem("rope_done")
        qk_turned = sem("qk_turned")
        qT_ready = sem("qT_ready")
        kT_ready = sem("kT_ready")
        scores_done = sem("scores_done")
        max_ready = sem("max_ready")
        neg_ready = sem("neg_ready")
        exp_done = sem("exp_done")
        inv_ready = sem("inv_ready")
        prob_ready = sem("prob_ready")
        prob_turned = sem("prob_turned")
        probT_ready = sem("probT_ready")
        pv_done = sem("pv_done")
        y_attn_ready = sem("y_attn_ready")
        attn_sq_ready = sem("attn_sq_ready")
        attn_sums_done = sem("attn_sums_done")
        y_attn_scaled = sem("y_attn_scaled")
        mix_done = sem("mix_done")
        mix_added = sem("mix_added")
        h2_ready = sem("h2_ready")
        h2_turned = sem("h2_turned")
        h2T_ready = sem("h2T_ready")
        logits_done = sem("logits_done")
        shifted_ready = sem("shifted_ready")
        aff_exp = sem("aff_exp")
        aff_ready = sem("aff_ready")
        aff_turned = sem("aff_turned")
        slot_row_ready = sem("slot_row_ready")
        slot_row_turned = sem("slot_row_turned")
        picks_ready = sem("picks_ready")
        gated_ready = sem("gated_ready")
        gathered = sem("gathered")
        gated_turned = sem("gated_turned")
        putT_ready = sem("putT_ready")
        xeT_ready = sem("xeT_ready")
        silu_ready = sem("silu_ready")
        hid_ready = sem("hid_ready")
        hid_turned = sem("hid_turned")
        hidT_ready = sem("hidT_ready")
        y_ready = sem("y_ready")
        put_done = sem("put_done")
        x_added = sem("x_added")
        final_ready = sem("final_ready")

        def load_front_slot(eng, n):
            if n < 12:
                col = W_IN_COLUMNS[n]
                src = w_in_d[0, :, col:col + 256].rearrange("(k p) c -> p k c", p=P)
                dst = ring[:, n, :].rearrange("p (k c) -> p k c", k=KD)
            else:
                row = 256 * (n - 12)
                src = w_out_d[0, row:row + 256, :].rearrange("(k p) c -> p k c", p=P)
                dst = ring[:, n, :].rearrange("p (k c) -> p k c", k=2)
            eng.dma_start(dst, src).then_inc(slot_loaded[n], 16)

        def expert_slot_source(e, i):
            if i < ROUNDS * ROUND_SLOTS:
                r, q = divmod(i, ROUND_SLOTS)
                w = (w_gate_d, w_up_d)[q % 2]
                row = 256 * (q // 2)
                src = w[0, e, row:row + 256, 1024 * r:1024 * r + 1024]
            else:
                row = 256 * (i - ROUNDS * ROUND_SLOTS)
                src = w_down_d[0, e, row:row + 256, :]
            return src.rearrange("(k p) c -> p k c", p=P)

        def slot_rows(i):
            return ring[:, i % RING, :].rearrange("p (k c) -> p k c", k=2)

        block = es.enter_context(nc.Block())

        @block.sync
        def _(sp):
            for t in range(NT):
                sp.dma_start(x_sb[:, t, :], x_d[0, P * t:P * t + P, :]).then_inc(x_loaded[t], 16)
            for n in range(FRONT_SLOTS):
                load_front_slot(sp, n)
            with sp.Fori(0, PAIRS) as pair:
                for i in range(PAIR_SLOTS):
                    sp.wait_ge(slots_used, pair * PAIR_SLOTS + (i + 1))
                    dst = slot_rows(i)
                    src = expert_slot_source(pair * 2 + i // EXPERT_SLOTS, i % EXPERT_SLOTS)
                    sp.dma_start(dst, src).then_inc(slot_loaded[i % RING], 16)
            for t in range(NT):
                sp.wait_ge(final_ready, t + 1)
                sp.dma_start(out_d[0, P * t:P * t + P, :], h2[:, t, :]).then_inc(out_stored, 16)
            sp.wait_ge(out_stored, 16 * NT)

        @block.gpsimd
        def _(pool):
            steps = [0]

            def step(ins):
                steps[0] += 1
                ins.then_inc(pool_step, 1)
                pool.wait_ge(pool_step, steps[0])

            step(pool.memset(ident[:, :], 0.0))
            pool.affine_select(out=ident[:, :], in_=ident[:, :], compare_op=ALU.not_equal, fill=1.0,
                               base=0, pattern=[[-1, P]], channel_multiplier=1).then_inc(consts_ready, 1)
            pool.memset(ones[:, :], 1.0).then_inc(consts_ready, 1)
            freqs = np.float32(ROPE_THETA) ** (-np.arange(ROT_HALF, dtype=np.float32) / np.float32(ROT_HALF))
            for i in range(ROT_HALF):
                pool.memset(inv_freq[:, i:i + 1], float(freqs[i])).then_inc(consts_ready, 1)
            pool.iota(dist.bitcast(I32), pattern=[[-1, 2 * S - P]], base=S - P,
                      channel_multiplier=1).then_inc(consts_ready, 1)
            pool.iota(slot_ids[:, :], pattern=[[1, CAP]], base=1, channel_multiplier=0,
                      allow_small_or_imprecise_dtypes=True).then_inc(consts_ready, 1)
            pool.wait_ge(xn_turned, 2 * NT)
            pool.wait_ge(strip_ready, 1)
            pool.memset(kT[64:128, 0], 0.0).then_inc(kT_zeroed, 1)
            pool.memset(kT[0:64, 1], 0.0).then_inc(kT_zeroed, 1)
            pool.wait_ge(kT_zeroed, 2)
            for m in range(KW):
                pool.wait_ge(y_conv_ready, m + 1)
                dst = conv_sq if m == 0 else conv_sq1
                step(pool.tensor_tensor(dst, yT_conv[:, m, :], yT_conv[:, m, :], ALU.mult))
                if m:
                    step(pool.tensor_tensor(conv_sq, conv_sq, conv_sq1, ALU.add))
            pool.sem_inc(conv_sq_ready, 1)
            pool.wait_ge(scores_done, 2 * UNITS)
            for m in range(KW):
                pool.wait_ge(y_attn_ready, NT * (m + 1))
                dst = attn_sq if m == 0 else attn_sq1
                step(pool.tensor_tensor(dst, yT_attn[:, m, :], yT_attn[:, m, :], ALU.mult))
                if m:
                    step(pool.tensor_tensor(attn_sq, attn_sq, attn_sq1, ALU.add))
            pool.sem_inc(attn_sq_ready, 1)

        @block.scalar
        def _(act):
            act.dma_start(g_mix, g_mix_d[0].partition_broadcast(P)).then_inc(g_mix_loaded, 16)
            act.dma_start(gain_rows[0:12, :], conv_w_d[0].rearrange("w (c p) -> (w c) p", p=P)).then_inc(rows_loaded, 16)
            act.dma_start(gain_rows[12:16, :], g_conv_d[0].rearrange("(c p) -> c p", p=P)).then_inc(rows_loaded, 16)
            act.dma_start(gain_rows[16:20, :], g_attn_d[0].rearrange("(c p) -> c p", p=P)).then_inc(rows_loaded, 16)
            act.dma_start(pos_int.bitcast(I32), positions_d[0].rearrange("(t p) -> t p", p=P)).then_inc(rows_loaded, 16)
            act.dma_start(router[:, :].rearrange("p (k e) -> p k e", k=KD),
                          w_router_d[0].rearrange("(k p) e -> p k e", p=P)).then_inc(router_loaded, 16)
            roots = [0]

            def root(width):
                n = roots[0]
                roots[0] += 1
                act.wait_ge(var_ready, n + 1)
                act.activation(norm[:, n, 1, 0:width], norm[:, n, 0, 0:width], ACT.Sqrt).then_inc(root_ready, 1)

            def turned_half(t):
                act.wait_ge(xn_turned, 2 * t + 1)
                act.activation(hT[:, 0:4, P * t:P * t + P],
                               bank[:, 2 * t, :].rearrange("p (k s) -> p k s", k=4), ACT.Copy).then_inc(hT_ready, 1)

            for t in range(NT):
                act.wait_ge(x_loaded[t], 16)
                act.activation(xn[:, t, :], x_sb[:, t, :], ACT.Square,
                               accum_out=sums[:, t:t + 1]).then_inc(squared, 1)
                root(1)
                if t:
                    turned_half(t - 1)
            turned_half(NT - 1)
            for m in range(KW):
                act.wait_ge(conv_done, 3 * m + 1)
                if m >= 2:
                    act.wait_ge(y_conv_ready, m - 1)
                act.activation(c_buf[m % 2], bank[:, 3 * (m % 2), :], ACT.Copy).then_inc(c_copied, 1)
                if m == 0:
                    act.wait_ge(turns_ready, 1)
                    act.activation(sin_cos[:, :], reduced[:, :], ACT.Sin).then_inc(sin_ready, 1)

            def qT_copy(t):
                act.wait_ge(qk_turned, 2 * t + 1)
                act.activation(qT[:, :, P * t:P * t + P],
                               bank[:, 6, :].rearrange("p (m s) -> p m s", m=KW), ACT.Copy).then_inc(qT_ready, 1)

            for t in range(NT):
                base = 3 * (t % 2)
                act.wait_ge(qkv_done, 3 * t + 2)
                if t >= 2:
                    act.wait_ge(qk_turned, 2 * (t - 1))
                act.activation(qk_stage[t % 2][:, 0:512], bank[:, base + 1, :], ACT.Copy,
                               scale=HEAD_DIM ** -0.5).then_inc(qk_copied, 1)
                act.wait_ge(qkv_done, 3 * t + 3)
                act.activation(qk_stage[t % 2][:, 512:1024], bank[:, base + 2, :], ACT.Copy).then_inc(qk_copied, 1)
                if t == 0:
                    root(NT)
                else:
                    qT_copy(t - 1)
            qT_copy(NT - 1)

            for i in range(UNITS + 2):
                if i < UNITS:
                    act.wait_ge(neg_ready, i + 1)
                    for h in range(2):
                        s = scores[i % 4][:, h, :]
                        c = 2 * i + h
                        act.activation(s, s, ACT.Exp, bias=neg_max[:, c:c + 1],
                                       accum_out=row_sum[:, c:c + 1]).then_inc(exp_done, 1)
                if i >= 2:
                    u = i - 2
                    act.wait_ge(prob_turned, u + 1)
                    act.activation(probT[u % 2].rearrange("p (b c) -> p b c", b=2), bank[:, 4:6, :],
                                   ACT.Copy).then_inc(probT_ready, 1)
            act.dma_start(x_sb, x_d[0].rearrange("(t p) d -> p t d", p=P)).then_inc(x_reloaded, 16)
            act.dma_start(g_ffn, g_ffn_d[0].partition_broadcast(P)).then_inc(gains_loaded, 16)
            act.dma_start(g_final, g_final_d.partition_broadcast(P)).then_inc(gains_loaded, 16)
            root(NT)

            for t in range(NT):
                act.wait_ge(mix_added, 2 * NT + 2 * t + 2)
                act.activation(h2[:, t, :], x_sb[:, t, :], ACT.Square,
                               accum_out=sums[:, NT + t:NT + t + 1]).then_inc(squared, 1)
                root(1)
                act.wait_ge(h2_turned, t + 1)
                b = 4 + 2 * (t % 2)
                act.activation(h2T[t % 2].rearrange("p (b c) -> p b c", b=2), bank[:, b:b + 2, :],
                               ACT.Copy).then_inc(h2T_ready, 1)
            act.wait_ge(shifted_ready, 1)
            act.activation(aff[:, :, :], aff[:, :, :], ACT.Exp).then_inc(aff_exp, 1)

            with act.Fori(0, PAIRS) as pair:
                act.wait_ge(gathered, pair * 2 + 1)
                act.activation(xeT[:, 0:4, :], bank[:, 6, :].rearrange("p (k s) -> p k s", k=4),
                               ACT.Copy).then_inc(xeT_ready, 1)
                for j in range(2):
                    for r in range(ROUNDS):
                        n = 2 * j + r
                        act.wait_ge(slots_used, pair * PAIR_SLOTS
                                    + (FRONT_SLOTS + EXPERT_SLOTS * j + ROUND_SLOTS * (r + 1)))
                        act.wait_ge(hid_ready, pair * 4 + (n + 1))
                        act.activation(silu[r], bank[:, r, :], ACT.Silu).then_inc(silu_ready, 1)
                    for r in range(ROUNDS):
                        act.wait_ge(hid_turned, pair * 4 + (2 * j + r + 1))
                        dst = hidT[:, 8 * r:8 * r + 8, :].rearrange("p (c b) s -> p b c s", c=2)
                        src = bank[:, 5, :].rearrange("p (b c s) -> p b c s", b=4, c=2)
                        act.activation(dst, src, ACT.Copy).then_inc(hidT_ready, 1)
                    act.wait_ge(slots_used, pair * PAIR_SLOTS + (FRONT_SLOTS + EXPERT_SLOTS * (j + 1)))
                    act.activation(y_pair[CAP * j:CAP * j + CAP, 0:512], bank[0:64, 4, :],
                                   ACT.Copy).then_inc(y_ready, 1)

            for t in range(NT):
                act.wait_ge(x_added, 2 * NT * (PAIRS - 1) + 2 * t + 2)
                act.activation(h2[:, t, :], x_sb[:, t, :], ACT.Square,
                               accum_out=sums[:, 2 * NT + t:2 * NT + t + 1]).then_inc(squared, 1)
                root(1)

        @block.vector
        def _(dve):
            steps = [0]
            norms = [0]

            def step(ins):
                steps[0] += 1
                ins.then_inc(dve_step, 1)
                dve.wait_ge(dve_step, steps[0])

            def inverse_root(total, count, width):
                n = norms[0]
                norms[0] += 1
                var, rt, inv, tmp = (norm[:, n, i, 0:width] for i in range(4))
                dve.tensor_scalar(var, total, 1.0 / count, RMS_EPS, ALU.mult, ALU.add).then_inc(var_ready, 1)
                dve.wait_ge(root_ready, n + 1)
                step(dve.reciprocal(inv, rt))
                step(dve.tensor_tensor(tmp, inv, inv, ALU.mult))
                step(dve.tensor_tensor(tmp, tmp, var, ALU.mult))
                step(dve.tensor_scalar(tmp, tmp, -0.5, 1.5, ALU.mult, ALU.add))
                step(dve.tensor_tensor(inv, inv, tmp, ALU.mult))
                return inv

            dve.wait_ge(rows_loaded, 64)
            dve.tensor_copy(pos_rows, pos_int.bitcast(I32)).then_inc(pos_ready, 1)
            dve.wait_ge(rows_turned, 2)
            dve.tensor_copy(columns[:, :], bank[:, 7, 0:24]).then_inc(columns_ready, 1)

            def turned_half(t):
                dve.wait_ge(xn_turned, 2 * t + 2)
                dve.tensor_copy(hT[:, 4:8, P * t:P * t + P],
                                bank[:, 2 * t + 1, :].rearrange("p (k s) -> p k s", k=4)).then_inc(hT_ready, 1)

            dve.wait_ge(g_mix_loaded, 16)
            for t in range(NT):
                dve.wait_ge(squared, t + 1)
                inv = inverse_root(sums[:, t:t + 1], D, 1)
                dve.scalar_tensor_tensor(out=xn[:, t, :], in0=x_sb[:, t, :], scalar=inv, in1=g_mix,
                                         op0=ALU.mult, op1=ALU.mult).then_inc(xn_ready, 1)
                if t:
                    turned_half(t - 1)
            turned_half(NT - 1)

            dve.wait_ge(consts_ready, 12)
            dve.wait_ge(columns_ready, 1)
            ang = angles[:, :].rearrange("p (t i) -> p t i", t=NT)
            step(dve.tensor_tensor(ang, columns[:, 20:24].unsqueeze(2).to_broadcast([P, NT, ROT_HALF]),
                                   inv_freq[:, :].unsqueeze(1).to_broadcast([P, NT, ROT_HALF]), ALU.mult))
            half = NT * ROT_HALF
            for i in range(2):
                step(dve.tensor_scalar(turns[:, half * i:half * i + half], angles[:, :],
                                       1.0 / (2.0 * math.pi), 0.25 * i, ALU.mult, ALU.add))
            step(dve.tensor_scalar(turns[:, :], turns[:, :], ROUND, None, ALU.add))
            step(dve.tensor_scalar(turns[:, :], turns[:, :], ROUND, None, ALU.subtract))
            for i in range(2):
                dst = reduced[:, half * i:half * i + half]
                src = angles[:, :]
                for part in TURN_PARTS:
                    step(dve.scalar_tensor_tensor(out=dst, in0=turns[:, half * i:half * i + half], scalar=-part,
                                                  in1=src, op0=ALU.mult, op1=ALU.add))
                    src = dst
            step(dve.tensor_scalar(reduced[:, half:2 * half], reduced[:, half:2 * half], math.pi / 2, None, ALU.add))
            dve.tensor_scalar(reduced[:, :], reduced[:, :], PI_INSIDE, -PI_INSIDE,
                              ALU.min, ALU.max).then_inc(turns_ready, 1)

            dist_i, a_i = dist.bitcast(I32), mask_a.bitcast(I32)
            step(dve.tensor_tensor(mask_b, dist_i, dist_i, ALU.mult))
            reach = [float((window // 2 // dil * dil) ** 2) for window, dil in PATTERNS]
            step(dve.tensor_scalar(strip[:, :], mask_b, reach[0], None, ALU.is_le))
            for (window, dil), far in list(zip(PATTERNS, reach))[1:]:
                step(dve.tensor_scalar(a_i, dist_i, dil - 1, None, ALU.bitwise_and))
                step(dve.tensor_scalar(mask_a, a_i, 0.0, None, ALU.is_equal))
                step(dve.scalar_tensor_tensor(out=mask_a, in0=mask_b, scalar=far, in1=mask_a,
                                              op0=ALU.is_le, op1=ALU.mult))
                step(dve.tensor_tensor(strip[:, :], strip[:, :], mask_a, ALU.add))
            step(dve.tensor_scalar(mask_a, strip[:, :], 2.0, math.log(2.0), ALU.is_equal, ALU.mult))
            step(dve.tensor_scalar(mask_b, strip[:, :], 3.0, math.log(3.0), ALU.is_equal, ALU.mult))
            step(dve.tensor_tensor(mask_a, mask_a, mask_b, ALU.add))
            step(dve.tensor_scalar(strip[:, :], strip[:, :], 0.0, MASKED, ALU.is_equal, ALU.mult))
            dve.tensor_tensor(strip[:, :], strip[:, :], mask_a, ALU.add).then_inc(strip_ready, 1)

            for b in range(2):
                step(dve.memset(z_buf[b][:, 0:1], 0.0))
                step(dve.memset(z_buf[b][:, S + 1:S + 2], 0.0))
            for m in range(KW):
                base = 3 * (m % 2)
                z = z_buf[m % 2]
                y = yT_conv[:, m, :]
                tap = [columns[:, KW * i + m:KW * i + m + 1] for i in range(TAPS)]
                dve.wait_ge(c_copied, m + 1)
                dve.wait_ge(conv_done, 3 * m + 2)
                step(dve.tensor_tensor(z[:, 1:S + 1], c_buf[m % 2], bank[:, base + 1, :], ALU.mult))
                step(dve.tensor_scalar(y, z[:, 0:S], tap[0], None, ALU.mult))
                step(dve.scalar_tensor_tensor(out=y, in0=z[:, 1:S + 1], scalar=tap[1], in1=y,
                                              op0=ALU.mult, op1=ALU.add))
                step(dve.scalar_tensor_tensor(out=y, in0=z[:, 2:S + 2], scalar=tap[2], in1=y,
                                              op0=ALU.mult, op1=ALU.add))
                dve.wait_ge(conv_done, 3 * m + 3)
                dve.tensor_tensor(y, y, bank[:, base + 2, :], ALU.mult).then_inc(y_conv_ready, 1)

            def kT_copy(t):
                dve.wait_ge(qk_turned, 2 * t + 2)
                if t == 0:
                    dve.wait_ge(kT_zeroed, 2)
                for h in range(2):
                    rows = slice(HEAD_DIM * h, HEAD_DIM * h + HEAD_DIM)
                    dve.tensor_copy(kT[rows, h, :, P * t:P * t + P],
                                    bank[rows, 7, :].rearrange("p (m s) -> p m s", m=KW)).then_inc(kT_ready, 1)

            for t in range(NT):
                base = 3 * (t % 2)
                dve.wait_ge(qkv_done, 3 * t + 1)
                dve.tensor_copy(v_sb[:, t, :], bank[:, base, :]).then_inc(v_copied, 1)
                if t == 0:
                    dve.wait_ge(conv_sums_done, NT)
                    inv_conv = inverse_root(bank[:, 6, 0:NT], W, NT)
                    dve.wait_ge(sin_ready, 1)
                heads = qk_stage[t % 2].rearrange("p (h c) -> p h c", c=HEAD_DIM)
                first, second = heads[:, :, 0:ROT_HALF], heads[:, :, ROT_HALF:2 * ROT_HALF]
                sin, cos = (sin_cos[:, half * i + ROT_HALF * t:half * i + ROT_HALF * t + ROT_HALF]
                            .unsqueeze(1).to_broadcast([P, 2 * NH, ROT_HALF]) for i in range(2))
                dve.wait_ge(qk_copied, 2 * t + 2)
                if t:
                    dve.wait_ge(rope_done, 2 * t)
                step(dve.tensor_tensor(rot[:, 0], first, cos, ALU.mult))
                step(dve.tensor_tensor(rot[:, 1], second, sin, ALU.mult))
                step(dve.tensor_tensor(rot[:, 2], second, cos, ALU.mult))
                step(dve.tensor_tensor(rot[:, 3], first, sin, ALU.mult))
                dve.tensor_tensor(first, rot[:, 0], rot[:, 1], ALU.subtract).then_inc(rope_done, 1)
                dve.tensor_tensor(second, rot[:, 2], rot[:, 3], ALU.add).then_inc(rope_done, 1)
                if t:
                    kT_copy(t - 1)
            kT_copy(NT - 1)
            dve.wait_ge(conv_sq_ready, 1)
            for m in range(KW):
                dve.tensor_scalar(yT_conv[:, m, :], yT_conv[:, m, :], columns[:, 12 + m:13 + m], None,
                                  ALU.mult).then_inc(y_conv_scaled, 1)

            def take_y(u):
                m, t = divmod(u, NT)
                dve.wait_ge(pv_done, u + 1)
                dve.tensor_copy(yT_attn[:, m, P * t:P * t + P], bank[:, 6 + u % 2, 0:P]).then_inc(y_attn_ready, 1)

            for i in range(UNITS + 1):
                if i < UNITS:
                    t = i % NT
                    seen = strip[:, S - P - P * t:2 * S - P - P * t]
                    for h in range(2):
                        c = 2 * i + h
                        dve.wait_ge(scores_done, c + 1)
                        dve.tensor_tensor_reduce(out=scores[i % 4][:, h, :], in0=bank[:, 2 * (i % 2) + h, :],
                                                 in1=seen, scale=1.0, scalar=-3e38, op0=ALU.add, op1=ALU.max,
                                                 accum_out=row_max[:, c:c + 1]).then_inc(max_ready, 1)
                    dve.wait_ge(max_ready, 2 * i + 2)
                    dve.tensor_scalar(neg_max[:, 2 * i:2 * i + 2], row_max[:, 2 * i:2 * i + 2], -1.0, None,
                                      ALU.mult).then_inc(neg_ready, 1)
                if i >= 1:
                    u = i - 1
                    dve.wait_ge(exp_done, 2 * u + 2)
                    dve.reciprocal(row_inv[:, 2 * u:2 * u + 2], row_sum[:, 2 * u:2 * u + 2]).then_inc(inv_ready, 1)
                    dve.wait_ge(inv_ready, u + 1)
                    for h in range(2):
                        s = scores[u % 4][:, h, :]
                        dve.tensor_scalar(s, s, row_inv[:, 2 * u + h:2 * u + h + 1], None,
                                          ALU.mult).then_inc(prob_ready, 1)
                if i >= 3:
                    take_y(i - 3)
            take_y(UNITS - 2)
            take_y(UNITS - 1)

            def add_mix(o, inv):
                t, n = divmod(o % (2 * NT), 2)
                xs = x_sb[:, t, B * n:B * n + B]
                dve.wait_ge(mix_done, o + 1)
                if o >= 2 * NT:
                    dve.wait_ge(mix_added, o - 2 * NT + 1)
                dve.scalar_tensor_tensor(out=xs, in0=bank[:, o % 3, :], scalar=inv[:, t:t + 1], in1=xs,
                                         op0=ALU.mult, op1=ALU.add).then_inc(mix_added, 1)

            dve.wait_ge(attn_sq_ready, 1)
            for m in range(KW):
                dve.tensor_scalar(yT_attn[:, m, :], yT_attn[:, m, :], columns[:, 16 + m:17 + m], None,
                                  ALU.mult).then_inc(y_attn_scaled, 1)
            dve.wait_ge(x_reloaded, 16)
            for o in range(4):
                add_mix(o, inv_conv)
            dve.wait_ge(attn_sums_done, NT)
            inv_attn = inverse_root(bank[:, 3, 256:256 + NT], W, NT)
            for o in range(4, 2 * NT):
                add_mix(o, inv_conv)
            dve.wait_ge(gains_loaded, 32)
            for t in range(NT):
                add_mix(2 * NT + 2 * t, inv_attn)
                add_mix(2 * NT + 2 * t + 1, inv_attn)
                dve.wait_ge(squared, NT + t + 1)
                inv = inverse_root(sums[:, NT + t:NT + t + 1], D, 1)
                dve.scalar_tensor_tensor(out=h2[:, t, :], in0=x_sb[:, t, :], scalar=inv, in1=g_ffn,
                                         op0=ALU.mult, op1=ALU.mult).then_inc(h2_ready, 1)

            logits = bank[:, 3, 0:NT * E].rearrange("p (t e) -> p t e", t=NT)
            dve.wait_ge(logits_done, NT)
            step(dve.tensor_reduce(small[:, 0, :], logits, AX.X, ALU.max))
            dve.tensor_tensor(aff[:, :, :], logits, small[:, 0, :].unsqueeze(2).to_broadcast([P, NT, E]),
                              ALU.subtract).then_inc(shifted_ready, 1)
            dve.wait_ge(aff_exp, 1)
            step(dve.tensor_reduce(small[:, 1, :], aff[:, :, :], AX.X, ALU.add))
            step(dve.reciprocal(small[:, 2, :], small[:, 1, :]))
            dve.tensor_tensor(aff[:, :, :], aff[:, :, :], small[:, 2, :].unsqueeze(2).to_broadcast([P, NT, E]),
                              ALU.mult).then_inc(aff_ready, 1)

            dve.wait_ge(aff_turned, NT)
            step(dve.tensor_copy(top_row[0], bank[0:E, 4, :]))
            for i in range(CAP // 8):
                step(dve.max(top8[:, :], top_row[i % 2]))
                step(dve.match_replace(out=top_row[(i + 1) % 2], in_to_replace=top8[:, :],
                                       in_values=top_row[i % 2], imm_value=-1.0))
            taken, other, chosen = top_row[(CAP // 8) % 2], top_row[(CAP // 8 + 1) % 2], top_row[2]
            step(dve.tensor_scalar(chosen, taken, -1.0, None, ALU.is_equal))
            step(dve.memset(other, 1.0))
            step(dve.tensor_tensor_scan(taken, other, chosen, 0.0, ALU.mult, ALU.add))
            dve.tensor_tensor(other, taken, chosen, ALU.mult).then_inc(slot_row_ready, 1)
            dve.wait_ge(slot_row_turned, NT)
            step(dve.tensor_copy(slot_of[:, :, :], bank[:, 5, 0:NT * E].rearrange("p (t e) -> p t e", t=NT)))
            dve.sem_inc(hid_ready, 2)

            with dve.Fori(0, PAIRS) as pair:
                places = slot_of[:, :, bass.ds(pair * 2, 2)]
                gates = aff[:, :, bass.ds(pair * 2, 2)]
                dve.tensor_tensor(picks, slot_ids[:, :].unsqueeze(1).unsqueeze(1).to_broadcast([P, NT, 2, CAP]),
                                  places.unsqueeze(3).to_broadcast([P, NT, 2, CAP]),
                                  ALU.is_equal).then_inc(picks_ready, 1)
                dve.wait_ge(picks_ready, pair + 1)
                dve.tensor_tensor(gated, picks, gates.unsqueeze(3).to_broadcast([P, NT, 2, CAP]),
                                  ALU.mult).then_inc(gated_ready, 1)
                dve.wait_ge(gathered, pair * 2 + 2)
                dve.tensor_copy(xeT[:, 4:8, :], bank[:, 7, :].rearrange("p (k s) -> p k s", k=4)).then_inc(xeT_ready, 1)
                dve.wait_ge(gated_turned, pair + 1)
                dve.tensor_copy(putT, bank[:, 5, :]).then_inc(putT_ready, 1)
                for j in range(2):
                    for r in range(ROUNDS):
                        dve.wait_ge(silu_ready, pair * 4 + (2 * j + r + 1))
                        dve.tensor_tensor(hid[r], silu[r], bank[:, 2 + r, :], ALU.mult).then_inc(hid_ready, 1)
                    dve.wait_ge(slots_used, pair * PAIR_SLOTS + (FRONT_SLOTS + EXPERT_SLOTS * (j + 1)))
                    dve.tensor_copy(y_pair[CAP * j:CAP * j + CAP, 512:1024], bank[64:128, 4, :]).then_inc(y_ready, 1)
                for o in range(2 * NT):
                    t, n = divmod(o, 2)
                    xs = x_sb[:, t, B * n:B * n + B]
                    dve.wait_ge(put_done, pair * (2 * NT) + (o + 1))
                    dve.tensor_tensor(xs, xs, bank[:, 6 + n, :], ALU.add).then_inc(x_added, 1)

            for t in range(NT):
                dve.wait_ge(squared, 2 * NT + t + 1)
                inv = inverse_root(sums[:, 2 * NT + t:2 * NT + t + 1], D, 1)
                dve.scalar_tensor_tensor(out=h2[:, t, :], in0=x_sb[:, t, :], scalar=inv, in1=g_final,
                                         op0=ALU.mult, op1=ALU.mult).then_inc(final_ready, 1)

        @block.tensor
        def _(pe):
            pe.wait_ge(consts_ready, 2)
            pe.wait_ge(rows_loaded, 64)
            pe.transpose(bank[:, 7, 0:20], gain_rows, ident[0:20, 0:20]).then_inc(rows_turned, 1)
            pe.wait_ge(pos_ready, 1)
            pe.transpose(bank[:, 7, 20:24], pos_rows, ident[0:NT, 0:NT]).then_inc(rows_turned, 1)

            for t in range(NT):
                pe.wait_ge(xn_ready, t + 1)
                if t == NT - 1:
                    pe.wait_ge(columns_ready, 1)
                for k in range(KD):
                    mm = pe.transpose(bank[:, 2 * t + k // 4, P * (k % 4):P * (k % 4) + P],
                                      xn[:, t, P * k:P * k + P], ident[:, :])
                    if k % 4 == 3:
                        mm.then_inc(xn_turned, 1)
            pe.wait_ge(hT_ready, 2 * NT)

            for m in range(KW):
                if m >= 2:
                    pe.wait_ge(y_conv_ready, m - 1)
                for i in range(3):
                    n = 3 * (m // 2) + i
                    pe.wait_ge(slot_loaded[n], 16)
                    w = ring[:, n, :].rearrange("p (k c) -> p k c", k=KD)
                    for k in range(KD):
                        mm = pe.matmul(bank[:, 3 * (m % 2) + i, :], w[:, k, P * (m % 2):P * (m % 2) + P],
                                       hT[:, k, :], start=(k == 0), stop=(k == KD - 1))
                        if m == 2 and i == 0 and k == 0:
                            mm.then_inc(slots_used, 3)
                    mm.then_inc(conv_done, 1)

            def qk_turn(t):
                pe.wait_ge(rope_done, 2 * t + 2)
                if t == 0:
                    pe.wait_ge(var_ready, NT + 1)
                    pe.wait_ge(hT_ready, 2 * NT)
                else:
                    pe.wait_ge(qT_ready, t)
                    pe.wait_ge(kT_ready, 2 * t)
                for i in range(2):
                    for m in range(KW):
                        mm = pe.transpose(bank[:, 6 + i, P * m:P * m + P],
                                          qk_stage[t % 2][:, 512 * i + P * m:512 * i + P * m + P], ident[:, :])
                        if t == NT - 1 and i == 0 and m == 0:
                            mm.then_inc(slots_used, 6)
                    mm.then_inc(qk_turned, 1)

            for t in range(NT):
                if t < 2:
                    pe.wait_ge(y_conv_ready, t + 3)
                else:
                    pe.wait_ge(v_copied, t - 1)
                    pe.wait_ge(qk_copied, 2 * (t - 1))
                for i in range(3):
                    n = 6 + 2 * i
                    pe.wait_ge(slot_loaded[n], 16)
                    pe.wait_ge(slot_loaded[n + 1], 16)
                    for k in range(KD):
                        mm = pe.matmul(bank[:, 3 * (t % 2) + i, :].rearrange("p (s c) -> p s c", s=2),
                                       hT[:, k, P * t:P * t + P], ring[:, n:n + 2, 256 * k:256 * k + 256],
                                       start=(k == 0), stop=(k == KD - 1))
                        if t == 0 and i == 0 and k == 0:
                            mm.then_inc(slots_used, 3)
                    mm.then_inc(qkv_done, 1)
                if t == 0:
                    pe.wait_ge(conv_sq_ready, 1)
                    for s in range(NT):
                        pe.matmul(bank[:, 6, s:s + 1], conv_sq[:, P * s:P * s + P], ones[:, :],
                                  start=True, stop=True).then_inc(conv_sums_done, 1)
                else:
                    qk_turn(t - 1)
            qk_turn(NT - 1)

            def unit_scores(u):
                m, t = divmod(u, NT)
                if u >= 2:
                    pe.wait_ge(max_ready, 2 * u - 2)
                for h in range(2):
                    pe.matmul(bank[:, 2 * (u % 2) + h, :], qT[:, m, P * t:P * t + P], kT[:, h, m, :],
                              start=True, stop=True).then_inc(scores_done, 1)

            pe.wait_ge(qT_ready, NT)
            pe.wait_ge(kT_ready, 2 * NT)
            pe.wait_ge(qk_copied, 2 * NT)
            pe.wait_ge(v_copied, NT)
            for u in range(3):
                unit_scores(u)
            for u in range(UNITS):
                m = u // NT
                pe.wait_ge(prob_ready, 2 * u + 2)
                if u:
                    pe.wait_ge(probT_ready, u)
                for h in range(2):
                    for k in range(NT):
                        mm = pe.transpose(bank[:, 4 + h, P * k:P * k + P],
                                          scores[u % 4][:, h, P * k:P * k + P], ident[:, :])
                mm.then_inc(prob_turned, 1)
                if u + 3 < UNITS:
                    unit_scores(u + 3)
                pe.wait_ge(probT_ready, u + 1)
                if u >= 2:
                    pe.wait_ge(y_attn_ready, u - 1)
                for k in range(NT):
                    for h in range(2):
                        head = 2 * m + h
                        mm = pe.matmul(bank[HEAD_DIM * h:HEAD_DIM * h + HEAD_DIM, 6 + u % 2, 0:P],
                                       v_sb[:, k, HEAD_DIM * head:HEAD_DIM * head + HEAD_DIM],
                                       probT[u % 2][:, 512 * h + P * k:512 * h + P * k + P],
                                       start=(k == 0), stop=(k == NT - 1))
                mm.then_inc(pv_done, 1)

            def mix_group(o):
                g, (t, n) = o // (2 * NT), divmod(o % (2 * NT), 2)
                yT = (yT_conv, yT_attn)[g]
                if o >= 3:
                    pe.wait_ge(mix_added, o - 2)
                for m in range(KW):
                    s = 12 + 2 * g + m // 2
                    if o in (0, 2 * NT):
                        pe.wait_ge(slot_loaded[s], 16)
                    mm = pe.matmul(bank[:, o % 3, :], yT[:, m, P * t:P * t + P],
                                   ring[:, s, 1024 * (m % 2) + B * n:1024 * (m % 2) + B * n + B],
                                   start=(m == 0), stop=(m == KW - 1))
                    if o == 2 * NT and m == 0:
                        mm.then_inc(slots_used, 2)
                mm.then_inc(mix_done, 1)

            def h2_turn_and_route(t):
                pe.wait_ge(h2_ready, t + 1)
                if t >= 2:
                    pe.wait_ge(h2T_ready, t - 1)
                b = 4 + 2 * (t % 2)
                for k in range(KD):
                    mm = pe.transpose(bank[:, b + k // 4, P * (k % 4):P * (k % 4) + P],
                                      h2[:, t, P * k:P * k + P], ident[:, :])
                    if t == NT - 1 and k == 0:
                        mm.then_inc(slots_used, 2)
                mm.then_inc(h2_turned, 1)
                pe.wait_ge(h2T_ready, t + 1)
                for k in range(KD):
                    mm = pe.matmul(bank[:, 3, E * t:E * t + E], h2T[t % 2][:, P * k:P * k + P],
                                   router[:, E * k:E * k + E], start=(k == 0), stop=(k == KD - 1))
                mm.then_inc(logits_done, 1)

            pe.wait_ge(max_ready, 2 * UNITS)
            pe.wait_ge(y_conv_scaled, KW)
            for o in range(2 * NT):
                mix_group(o)
                if o == 2:
                    pe.wait_ge(attn_sq_ready, 1)
                    for s in range(NT):
                        pe.matmul(bank[:, 3, 256 + s:257 + s], attn_sq[:, P * s:P * s + P], ones[:, :],
                                  start=True, stop=True).then_inc(attn_sums_done, 1)
            pe.wait_ge(y_attn_scaled, KW)
            pe.wait_ge(router_loaded, 16)
            pe.wait_ge(y_attn_ready, UNITS)
            for t in range(NT):
                mix_group(2 * NT + 2 * t)
                mix_group(2 * NT + 2 * t + 1)
                if t:
                    h2_turn_and_route(t - 1)
            h2_turn_and_route(NT - 1)

            pe.wait_ge(aff_ready, 1)
            for t in range(NT):
                pe.transpose(bank[0:E, 4, P * t:P * t + P], aff[:, t, :], ident[:, :]).then_inc(aff_turned, 1)
            pe.wait_ge(slot_row_ready, 1)
            place_row = top_row[(CAP // 8 + 1) % 2]
            for t in range(NT):
                pe.transpose(bank[:, 5, E * t:E * t + E], place_row[:, P * t:P * t + P],
                             ident[0:E, 0:E]).then_inc(slot_row_turned, 1)

            with pe.Fori(0, PAIRS) as pair:
                pe.wait_ge(picks_ready, pair + 1)
                for k in range(KD):
                    for t in range(NT):
                        mm = pe.matmul(bank[:, 6 + k // 4, P * (k % 4):P * (k % 4) + P],
                                       h2[:, t, P * k:P * k + P], picks[:, t, :, :].rearrange("p j s -> p (j s)"),
                                       start=(t == 0), stop=(t == NT - 1))
                    if k % 4 == 3:
                        mm.then_inc(gathered, 1)
                pe.wait_ge(gated_ready, pair + 1)
                for t in range(NT):
                    mm = pe.transpose(bank[:, 5, P * t:P * t + P],
                                      gated[:, t, :, :].rearrange("p j s -> p (j s)"), ident[:, :])
                mm.then_inc(gated_turned, 1)
                pe.wait_ge(xeT_ready, pair * 2 + 2)
                for j in range(2):
                    tokens = slice(CAP * j, CAP * j + CAP)
                    for r in range(ROUNDS):
                        pe.wait_ge(hid_ready, pair * 4 + (2 * j + r + 1))
                        for q in range(ROUND_SLOTS):
                            i = EXPERT_SLOTS * j + ROUND_SLOTS * r + q
                            pe.wait_ge(slot_loaded[i % RING], pair * (16 * PAIR_SLOTS // RING) + 16 * (i // RING + 2))
                            for kk in range(2):
                                k = 2 * (q // 2) + kk
                                for c in range(2):
                                    mm = pe.matmul(bank[64 * c:64 * c + 64, 2 * (q % 2) + r, :], xeT[:, k, tokens],
                                                   slot_rows(i)[:, kk, B * c:B * c + B],
                                                   start=(k == 0), stop=(k == KD - 1))
                            mm.then_inc(slots_used, 1)
                    for r in range(ROUNDS):
                        pe.wait_ge(hid_ready, pair * 4 + (2 * j + r + 3))
                        if r == 0 and j == 0:
                            pe.wait_ge(putT_ready, pair + 1)
                        else:
                            pe.wait_ge(hidT_ready, pair * 4 + (2 * j + r))
                        for b in range(4):
                            mm = pe.transpose(bank[:, 5, P * b:P * b + P], hid[r][:, P * b:P * b + P], ident[:, :])
                        mm.then_inc(hid_turned, 1)
                    if j:
                        pe.wait_ge(y_ready, pair * 4 + 2)
                    pe.wait_ge(hidT_ready, pair * 4 + (2 * j + 2))
                    for q in range(F // 256):
                        i = EXPERT_SLOTS * j + ROUNDS * ROUND_SLOTS + q
                        pe.wait_ge(slot_loaded[i % RING], pair * (16 * PAIR_SLOTS // RING) + 16 * (i // RING + 2))
                        for kk in range(2):
                            f = 2 * q + kk
                            for c in range(2):
                                mm = pe.matmul(bank[64 * c:64 * c + 64, 4, :], hidT[:, f, :],
                                               slot_rows(i)[:, kk, B * c:B * c + B],
                                               start=(f == 0), stop=(f == F // P - 1))
                        mm.then_inc(slots_used, 1)
                pe.wait_ge(y_ready, pair * 4 + 4)
                for o in range(2 * NT):
                    t, n = divmod(o, 2)
                    if o >= 2:
                        pe.wait_ge(x_added, pair * (2 * NT) + (o - 1))
                    pe.matmul(bank[:, 6 + n, :], putT[:, P * t:P * t + P], y_pair[:, B * n:B * n + B],
                              start=True, stop=True).then_inc(put_done, 1)
                pe.wait_ge(x_added, (pair + 1) * (2 * NT))


_INS = ["x", "positions", "g_mix", "w_in", "conv_w", "g_conv_out", "g_attn_out", "w_out", "g_ffn", "w_router",
        "w_gate", "w_up", "w_down", "g_final"]


def kernel(**inputs):
    import concourse.bacc as bacc
    from concourse.bass_utils import run_bass_kernel_spmd

    nc = bacc.Bacc("TRN2", target_bir_lowering=False, num_devices=1)
    arrays, args = {}, []
    for name in _INS:
        a = np.ascontiguousarray(inputs[name])
        arrays[f"in_{name}"] = a
        args.append(nc.dram_tensor(f"in_{name}", a.shape, mybir.dt.from_np(a.dtype), kind="ExternalInput").ap())
    out = nc.dram_tensor("out_0", inputs["x"].shape, F32, kind="ExternalOutput").ap()
    hybrid_layer(nc, *args, out)
    r = run_bass_kernel_spmd(nc, [arrays], core_ids=[0])
    return r.results[0]["out_0"]
```

```python
import math
from contextlib import ExitStack

import numpy as np

import concourse.bass as bass
from concourse import mybir

P = 128
F32 = mybir.dt.float32
F32R = mybir.dt.float32r
I32 = mybir.dt.int32
ALU = mybir.AluOpType
ACT = mybir.ActivationFunctionType
AX = mybir.AxisListType

HEAD_DIM = 64
ROT_HALF = HEAD_DIM // 8
ROPE_THETA = 500000.0
RMS_EPS = 1e-6
MASKED = -1e30
CAPACITY_FACTOR = 2
PATTERNS = ((128, 1), (512, 4), (2048, 16))

def turn_parts(bits, count):
    left, parts = 2.0 * math.pi, []
    for _ in range(count):
        unit = 2.0 ** (math.floor(math.log2(left)) + 1 - bits)
        parts.append(math.floor(left / unit) * unit)
        left -= parts[-1]
    return (*parts, left)


TURN_PARTS = turn_parts(10, 3)
ROUND = 12582912.0
PI_INSIDE = 3.1415925


def hybrid_layer(nc, x_d, positions_d, g_mix_d, w_in_d, conv_w_d, g_conv_d, g_attn_d, w_out_d,
                 g_ffn_d, w_router_d, w_gate_d, w_up_d, w_down_d, g_final_d, out_d):
    _, S, D = x_d.shape
    _, E, _, F = w_gate_d.shape
    W = D // 2
    NT = S // P
    KD = D // P
    KW = W // P
    NH = W // HEAD_DIM
    CAP = CAPACITY_FACTOR * S // E
    B = 512
    ROUNDS = F // (2 * B)
    PAIRS = E // 2
    TAPS = conv_w_d.shape[1]
    assert S == B and D == 2 * B and CAP == 64 and NH == 2 * KW and TAPS == 3

    RING = 16
    SLOT = 2048
    FRONT_USES = RING
    ROUND_SLOTS = 2 * (D // 256)
    EXPERT_SLOTS = ROUNDS * ROUND_SLOTS + F // 256
    PAIR_SLOTS = 2 * EXPERT_SLOTS
    assert PAIR_SLOTS % RING == 0

    PIECE = 1024
    V, Q, K, CONV, OUT = 0, 1, 2, 3, 3 + KW
    PIECES = [4] * CONV + [3] * KW + [4] * 2
    UNITS = KW * NT

    with ExitStack() as es:
        def sb(name, shape, dt=F32):
            return es.enter_context(nc.sbuf_tensor(name, shape, dt))

        def sem(name):
            return es.enter_context(nc.semaphore(name))

        ring_base = -(-nc.sbuf_base // 32) * 32
        ring_flat = sb("ring_flat", [P, RING * SLOT])
        desk = sb("desk", [P, 9 * SLOT + 2])
        ring = ring_flat[:, :].rearrange("p (s c) -> p s c", s=RING)

        def block_of(n, count=1):
            if n < RING:
                return ring_flat[:, SLOT * n:SLOT * (n + count)]
            return desk[:, SLOT * (n - RING):SLOT * (n - RING + count)]

        def split_blocks(name, n, count):
            return nc.alloc_sbuf_tensor_at(name, [P, SLOT * count], F32R, offset=ring_base + 4 * SLOT * n)

        PLACES = (0, 8, 12)
        lo_raw = [block_of(b, 2) for b in PLACES]
        unit_split = [split_blocks(f"unit_split{g}", b, 4) for g, b in enumerate(PLACES)]
        w_lo = [split[:, 0:2 * SLOT] for split in unit_split]
        w_hi = [split[:, 2 * SLOT:4 * SLOT] for split in unit_split]
        h_split = split_blocks("h_split", 4, 4)
        hT_hi = h_split[:, 0:2 * SLOT].rearrange("p (k t) -> p k t", k=KD)
        hT_lo = h_split[:, 2 * SLOT:4 * SLOT].rearrange("p (k t) -> p k t", k=KD)
        yc_hi = h_split[:, 2 * SLOT:3 * SLOT].rearrange("p (m t) -> p m t", m=KW)
        yc_lo = h_split[:, 3 * SLOT:4 * SLOT].rearrange("p (m t) -> p m t", m=KW)
        r1 = block_of(16)
        mask_b = r1[:, 0:896]
        probT = [r1[:, 1024 * b:1024 * b + 1024] for b in range(2)]
        x2T = probT
        xeT = r1[:, 0:1024].rearrange("p (k s) -> p k s", k=KD)
        hidT = r1[:, 1024:2048].rearrange("p (f s) -> p f s", s=CAP)
        rows = block_of(17)
        gain_rows, mix_rows = rows[0:28, 0:128], rows[0:KD, 128:256]
        pos_int, pos_rows = rows[0:NT, 256:384], rows[0:NT, 384:512]
        yT_conv = rows.rearrange("p (m t) -> p m t", m=KW)
        yT_attn = block_of(18).rearrange("p (m t) -> p m t", m=KW)
        dist, mask_a = block_of(18)[:, 0:896], block_of(18)[:, 896:1792]
        h2 = block_of(17, 2).rearrange("p (t d) -> p t d", t=NT)
        r3 = block_of(19)
        v_sb = r3.rearrange("p (t c) -> p t c", t=NT)
        top_row = [r3[0:E, 512 * b:512 * b + 512] for b in range(3)]
        silu = [r3[:, 512 * b:512 * b + 512] for b in range(2)]
        hid = [r3[:, 1024 + 512 * b:1536 + 512 * b] for b in range(2)]
        r4 = block_of(20)
        qT = r4.rearrange("p (m t) -> p m t", m=KW)
        g_ffn = r4[:, 0:1024]
        attn_sq, attn_sq1 = r4[:, 1024:1536], r4[:, 1536:2048]
        y_pair = r4[:, 0:1024]
        gated = r4[:, 1024:1536].rearrange("p (t j s) -> p t j s", t=NT, j=2)
        putT = r4[:, 1536:2048]
        xn = block_of(21, 2).rearrange("p (t d) -> p t d", t=NT)
        kT = block_of(21, 2).rearrange("p (h m t) -> p h m t", h=2, m=KW)
        ya_split = split_blocks("ya_split", 21, 2)
        ya_hi = ya_split[:, 0:SLOT].rearrange("p (m t) -> p m t", m=KW)
        ya_lo = ya_split[:, SLOT:2 * SLOT].rearrange("p (m t) -> p m t", m=KW)
        g_final = block_of(21)[:, 0:D]
        ZW = S + 2
        x_reg = desk[:, 7 * SLOT:9 * SLOT + 2]
        x_sb = x_reg[:, 0:NT * D].rearrange("p (t d) -> p t d", t=NT)
        STAGES = 3
        stage = [x_reg[:, 512 * b:512 * b + 512] for b in range(STAGES)]
        rot = x_reg[:, 2048:2304].rearrange("p (i h c) -> p i h c", i=4, h=NH)
        z_buf = [x_reg[:, b:b + ZW] for b in (2048, 0)]
        c_buf = [x_reg[:, b + ZW:b + ZW + S] for b in (2048, 0)]
        conv_sq, conv_sq1 = x_reg[:, 3074:3586], x_reg[:, 3586:4098]
        scores = [x_reg[:, 1024 * b:1024 * b + 1024].rearrange("p (h k) -> p h k", h=2) for b in range(3)]
        strip = sb("strip", [P, 2 * S - P])
        picks = strip[:, 0:512].rearrange("p (t j s) -> p t j s", t=NT, j=2)
        ident = sb("ident", [P, P])
        ones = sb("ones", [P, 1])
        slot_ids = sb("slot_ids", [P, CAP])
        router_wide = sb("router_wide", [P, KD * E + 96 - E])
        router = router_wide[:, 0:KD * E]
        inv_freq = sb("inv_freq", [P, ROT_HALF])
        angles = sb("angles", [P, NT * ROT_HALF])
        turns = sb("turns", [P, 2 * NT * ROT_HALF])
        reduced = sb("reduced", [P, 2 * NT * ROT_HALF])
        sin_cos = sb("sin_cos", [P, 2 * NT * ROT_HALF])
        mix_gains = sb("mix_gains", [P, KD])
        columns = sb("columns", [P, 32])
        sums = sb("sums", [P, 3 * NT])
        norm = sb("norm", [P, 4, 4, 2 * NT])
        row_max = sb("row_max", [P, 2 * UNITS])
        neg_max = sb("neg_max", [P, 2 * UNITS])
        row_sum = sb("row_sum", [P, 2 * UNITS])
        row_inv = sb("row_inv", [P, 2 * UNITS])
        aff = sb("aff", [P, NT, E])
        slot_of = sb("slot_of", [P, NT, E])
        small = sb("small", [P, 4, NT])
        top8 = sb("top8", [E, 8])
        bank = es.enter_context(nc.psum_tensor("bank", [P, 8, B], F32))

        x_loaded = [sem(f"x_loaded{t}") for t in range(NT)]
        g_mix_loaded = sem("g_mix_loaded")
        rows_loaded = sem("rows_loaded")
        router_loaded = sem("router_loaded")
        router_scaled = sem("router_scaled")
        x_reloaded = sem("x_reloaded")
        g_ffn_loaded = sem("g_ffn_loaded")
        g_final_loaded = sem("g_final_loaded")
        unit_loaded = [sem(f"unit{u}_loaded") for u in range(len(PIECES))]
        v_rest_loaded = sem("v_rest_loaded")
        hi_ready = sem("hi_ready")
        lo_ready = sem("lo_ready")
        out_lo_ready = sem("out_lo_ready")
        mix_gains_turned = sem("mix_gains_turned")
        mix_gains_ready = sem("mix_gains_ready")
        hT_hi_ready = sem("hT_hi_ready")
        yc_hi_ready = sem("yc_hi_ready")
        ya_hi_ready = sem("ya_hi_ready")
        slot_loaded = [sem(f"slot_loaded{s}") for s in range(RING)]
        slots_used = sem("slots_used")
        out_stored = sem("out_stored")
        pool_step = sem("pool_step")
        consts_ready = sem("consts_ready")
        pos_ready = sem("pos_ready")
        rows_turned = sem("rows_turned")
        columns_ready = sem("columns_ready")
        dve_step = sem("dve_step")
        squared = sem("squared")
        var_ready = sem("var_ready")
        root_ready = sem("root_ready")
        xn_ready = sem("xn_ready")
        xn_turned = sem("xn_turned")
        hT_lo_ready = sem("hT_lo_ready")
        strip_ready = sem("strip_ready")
        turns_ready = sem("turns_ready")
        sin_ready = sem("sin_ready")
        kT_zeroed = sem("kT_zeroed")
        conv_done = sem("conv_done")
        c_copied = sem("c_copied")
        y_conv_ready = sem("y_conv_ready")
        conv_sq_ready = sem("conv_sq_ready")
        yc_lo_ready = sem("yc_lo_ready")
        qkv_done = sem("qkv_done")
        item_copied = sem("item_copied")
        rope_done = sem("rope_done")
        qk_turned = sem("qk_turned")
        qT_ready = sem("qT_ready")
        kT_ready = sem("kT_ready")
        scores_done = sem("scores_done")
        max_ready = sem("max_ready")
        neg_ready = sem("neg_ready")
        exp_done = sem("exp_done")
        inv_ready = sem("inv_ready")
        prob_ready = sem("prob_ready")
        prob_turned = sem("prob_turned")
        probT_ready = sem("probT_ready")
        pv_done = sem("pv_done")
        y_attn_ready = sem("y_attn_ready")
        attn_sq_ready = sem("attn_sq_ready")
        attn_sums_done = sem("attn_sums_done")
        ya_lo_ready = sem("ya_lo_ready")
        mix_done = sem("mix_done")
        mix_added = sem("mix_added")
        h2_ready = sem("h2_ready")
        x2_turned = sem("x2_turned")
        x2T_ready = sem("x2T_ready")
        logits_done = sem("logits_done")
        shifted_ready = sem("shifted_ready")
        aff_exp = sem("aff_exp")
        aff_ready = sem("aff_ready")
        aff_turned = sem("aff_turned")
        slot_row_ready = sem("slot_row_ready")
        slot_row_turned = sem("slot_row_turned")
        picks_ready = sem("picks_ready")
        gated_ready = sem("gated_ready")
        gathered = sem("gathered")
        gated_turned = sem("gated_turned")
        putT_ready = sem("putT_ready")
        xeT_ready = sem("xeT_ready")
        silu_ready = sem("silu_ready")
        hid_ready = sem("hid_ready")
        hid_turned = sem("hid_turned")
        hidT_ready = sem("hidT_ready")
        y_ready = sem("y_ready")
        put_done = sem("put_done")
        x_added = sem("x_added")
        gained = sem("gained")
        final_ready = sem("final_ready")

        def unit_piece(u, c, place):
            return place[u % 3][:, PIECE * c:PIECE * c + PIECE]

        def pieces_before(u):
            return sum(PIECES[:u])

        def unit_k(u, k, place):
            return place[u % 3][:, W * k:W * k + W]

        def expert_slot_source(e, i):
            if i < ROUNDS * ROUND_SLOTS:
                r, q = divmod(i, ROUND_SLOTS)
                w = (w_gate_d, w_up_d)[q % 2]
                row = 256 * (q // 2)
                src = w[0, e, row:row + 256, 1024 * r:1024 * r + 1024]
            else:
                row = 256 * (i - ROUNDS * ROUND_SLOTS)
                src = w_down_d[0, e, row:row + 256, :]
            return src.rearrange("(k p) c -> p k c", p=P)

        def slot_rows(i):
            return ring[:, i % RING, :].rearrange("p (k c) -> p k c", k=2)

        def turned_h(t, k):
            return bank[:, 6 - 2 * (t % 2) + k // 4, P * (k % 4):P * (k % 4) + P]

        def conv_bank(m):
            return 3 - 3 * (m % 2)

        block = es.enter_context(nc.Block())

        @block.sync
        def _(sp):
            def load_x(t):
                sp.dma_start(x_sb[:, t, :], x_d[0, P * t:P * t + P, :]).then_inc(x_loaded[t], 16)

            def load_rows(u, k0, k1, loaded):
                col = (5 * W, 3 * W, 4 * W)[u]
                src = w_in_d[0, P * k0:P * k1, col:col + W].rearrange("(k p) c -> p k c", p=P)
                dst = lo_raw[u % 3][:, W * k0:W * k1].rearrange("p (k c) -> p k c", c=W)
                sp.dma_start(dst, src).then_inc(loaded, 16)

            load_x(0)
            load_x(1)
            load_rows(V, 0, 4, unit_loaded[V])
            load_rows(V, 4, 8, v_rest_loaded)
            load_x(2)
            load_x(3)
            load_rows(Q, 0, 8, unit_loaded[Q])
            load_rows(K, 0, 8, unit_loaded[K])
            for m in range(KW):
                u = CONV + m
                if m < CONV:
                    sp.wait_ge(qkv_done, NT * (m + 1))
                else:
                    sp.wait_ge(conv_done, 3 * (m - CONV + 1))
                for c, part in enumerate((1, 2, 0)):
                    col = W * part + P * m
                    src = w_in_d[0, :, col:col + P].rearrange("(k p) c -> p k c", p=P)
                    dst = unit_piece(u, c, lo_raw).rearrange("p (k c) -> p k c", k=KD)
                    sp.dma_start(dst, src).then_inc(unit_loaded[u], 16)
            for g in range(2):
                u = OUT + g
                sp.wait_ge(conv_done, 3 * (u - 3 - CONV + 1))
                src = w_out_d[0, W * g:W * g + W, :].rearrange("(k p) c -> p k c", p=P)
                dst = lo_raw[u % 3].rearrange("p (k c) -> p k c", k=KW)
                sp.dma_start(dst, src).then_inc(unit_loaded[u], 16)
            with sp.Fori(0, PAIRS) as pair:
                for i in range(PAIR_SLOTS):
                    sp.wait_ge(slots_used, pair * PAIR_SLOTS + (i + 1))
                    dst = slot_rows(i)
                    src = expert_slot_source(pair * 2 + i // EXPERT_SLOTS, i % EXPERT_SLOTS)
                    sp.dma_start(dst, src).then_inc(slot_loaded[i % RING], 16)
            for t in range(NT):
                sp.wait_ge(final_ready, t + 1)
                sp.dma_start(out_d[0, P * t:P * t + P, :], h2[:, t, :]).then_inc(out_stored, 16)
            sp.wait_ge(out_stored, 16 * NT)

        @block.gpsimd
        def _(pool):
            steps = [0]

            def step(ins):
                steps[0] += 1
                ins.then_inc(pool_step, 1)
                pool.wait_ge(pool_step, steps[0])

            step(pool.memset(ident[:, :], 0.0))
            pool.affine_select(out=ident[:, :], in_=ident[:, :], compare_op=ALU.not_equal, fill=1.0,
                               base=0, pattern=[[-1, P]], channel_multiplier=1).then_inc(consts_ready, 1)
            pool.memset(ones[:, :], 1.0).then_inc(consts_ready, 1)
            freqs = np.float32(ROPE_THETA) ** (-np.arange(ROT_HALF, dtype=np.float32) / np.float32(ROT_HALF))
            for i in range(ROT_HALF):
                pool.memset(inv_freq[:, i:i + 1], float(freqs[i])).then_inc(consts_ready, 1)
            pool.iota(dist.bitcast(I32), pattern=[[-1, 2 * S - P]], base=S - P,
                      channel_multiplier=1).then_inc(consts_ready, 1)
            pool.memset(router_wide[:, KD * E:], 0.0).then_inc(consts_ready, 1)
            pool.iota(slot_ids[:, :], pattern=[[1, CAP]], base=1, channel_multiplier=0,
                      allow_small_or_imprecise_dtypes=True).then_inc(consts_ready, 1)
            pool.wait_ge(consts_ready, 13)
            pool.wait_ge(xn_turned, 2 * NT)
            pool.memset(kT[64:128, 0], 0.0).then_inc(kT_zeroed, 1)
            pool.memset(kT[0:64, 1], 0.0).then_inc(kT_zeroed, 1)
            pool.wait_ge(kT_zeroed, 2)
            for m in range(KW):
                pool.wait_ge(y_conv_ready, m + 1)
                dst = conv_sq if m == 0 else conv_sq1
                step(pool.tensor_tensor(dst, yT_conv[:, m, :], yT_conv[:, m, :], ALU.mult))
                if m:
                    step(pool.tensor_tensor(conv_sq, conv_sq, conv_sq1, ALU.add))
            pool.sem_inc(conv_sq_ready, 1)
            for u in (OUT, OUT + 1):
                for c in range(PIECES[u]):
                    pool.wait_ge(hi_ready, pieces_before(u) + c + 1)
                    pool.tensor_tensor(unit_piece(u, c, w_lo), unit_piece(u, c, lo_raw),
                                       unit_piece(u, c, w_hi).bitcast(F32), ALU.subtract).then_inc(out_lo_ready, 1)
            pool.wait_ge(out_lo_ready, PIECES[OUT] + PIECES[OUT + 1])
            pool.wait_ge(scores_done, 2 * UNITS)
            for m in range(KW):
                pool.wait_ge(y_attn_ready, NT * (m + 1))
                dst = attn_sq if m == 0 else attn_sq1
                step(pool.tensor_tensor(dst, yT_attn[:, m, :], yT_attn[:, m, :], ALU.mult))
                if m:
                    step(pool.tensor_tensor(attn_sq, attn_sq, attn_sq1, ALU.add))
            pool.sem_inc(attn_sq_ready, 1)
            pool.wait_ge(g_final_loaded, 16)
            for t in range(NT):
                pool.wait_ge(x_added, 2 * NT * (PAIRS - 1) + 2 * t + 2)
                pool.tensor_tensor(h2[:, t, :], x_sb[:, t, :], g_final, ALU.mult).then_inc(gained, 1)

        @block.scalar
        def _(act):
            act.dma_start(mix_rows, g_mix_d[0].rearrange("(c p) -> c p", p=P)).then_inc(g_mix_loaded, 16)
            act.dma_start(gain_rows[0:12, :], conv_w_d[0].rearrange("w (c p) -> (w c) p", p=P)).then_inc(rows_loaded, 16)
            act.dma_start(gain_rows[12:16, :], g_conv_d[0].rearrange("(c p) -> c p", p=P)).then_inc(rows_loaded, 16)
            act.dma_start(gain_rows[16:20, :], g_attn_d[0].rearrange("(c p) -> c p", p=P)).then_inc(rows_loaded, 16)
            act.dma_start(gain_rows[20:28, :], g_ffn_d[0].rearrange("(c p) -> c p", p=P)).then_inc(rows_loaded, 16)
            act.dma_start(pos_int.bitcast(I32), positions_d[0].rearrange("(t p) -> t p", p=P)).then_inc(rows_loaded, 16)
            roots = [0]

            def root(width):
                n = roots[0]
                roots[0] += 1
                act.wait_ge(var_ready, n + 1)
                act.activation(norm[:, n % 4, 1, 0:width], norm[:, n % 4, 0, 0:width], ACT.Sqrt).then_inc(root_ready, 1)

            def square(t):
                act.wait_ge(x_loaded[t], 16)
                act.activation(xn[:, t, :], x_sb[:, t, :], ACT.Square,
                               accum_out=sums[:, t:t + 1]).then_inc(squared, 1)

            def unit_hi(u, c0, c1):
                for c in range(c0, c1):
                    if c == c0:
                        act.wait_ge(unit_loaded[u], 16 * (3 if CONV <= u < OUT else 1))
                    if (u, c) == (V, 2):
                        act.wait_ge(v_rest_loaded, 16)
                    act.activation(unit_piece(u, c, w_hi), unit_piece(u, c, lo_raw), ACT.Copy).then_inc(hi_ready, 1)

            def hT_hi_make(t):
                act.wait_ge(mix_gains_ready, 1)
                for i in range(2):
                    act.wait_ge(xn_turned, 2 * t + i + 1)
                    for k in range(4 * i, 4 * i + 4):
                        ins = act.activation(hT_hi[:, k, P * t:P * t + P], turned_h(t, k), ACT.Copy,
                                             scale=mix_gains[:, k:k + 1])
                    ins.then_inc(hT_hi_ready, 1)

            def v_copy(t):
                act.wait_ge(qkv_done, t + 1)
                act.activation(v_sb[:, t, :], bank[:, t % 3, :], ACT.Copy).then_inc(item_copied, 1)

            def qk_copy(j):
                n = NT + j
                act.wait_ge(qkv_done, n + 1)
                if j == 0:
                    act.wait_ge(xn_ready, NT)
                if j >= STAGES:
                    act.wait_ge(qk_turned, j - STAGES + 1)
                act.activation(stage[j % STAGES], bank[:, n % 3, :], ACT.Copy,
                               scale=HEAD_DIM ** -0.5 if j < NT else 1.0).then_inc(item_copied, 1)

            def qT_copy(t):
                act.wait_ge(qk_turned, t + 1)
                act.activation(qT[:, :, P * t:P * t + P],
                               bank[:, 6 + t % 2, :].rearrange("p (m s) -> p m s", m=KW), ACT.Copy).then_inc(qT_ready, 1)

            def c_copy(m):
                act.wait_ge(conv_done, 3 * m + 1)
                if m >= 2:
                    act.wait_ge(y_conv_ready, m - 1)
                act.activation(c_buf[m % 2], bank[:, conv_bank(m), :], ACT.Copy).then_inc(c_copied, 1)

            square(0)
            root(1)
            square(1)
            root(1)
            hT_hi_make(0)
            unit_hi(V, 0, 2)
            hT_hi_make(1)
            unit_hi(V, 2, 4)
            square(2)
            root(1)
            v_copy(0)
            hT_hi_make(2)
            square(3)
            root(1)
            v_copy(1)
            hT_hi_make(3)
            unit_hi(Q, 0, 4)
            v_copy(2)
            act.wait_ge(turns_ready, 1)
            act.activation(sin_cos[:, :], reduced[:, :], ACT.Sin).then_inc(sin_ready, 1)
            v_copy(3)
            act.dma_start(router[:, :].rearrange("p (k e) -> p k e", k=KD),
                          w_router_d[0].rearrange("(k p) e -> p k e", p=P)).then_inc(router_loaded, 16)
            qk_copy(0)
            unit_hi(K, 0, 2)
            qk_copy(1)
            qT_copy(0)
            unit_hi(K, 2, 4)
            qk_copy(2)
            qT_copy(1)
            qk_copy(3)
            qT_copy(2)
            unit_hi(CONV, 0, 3)
            qk_copy(4)
            qT_copy(3)
            qk_copy(5)
            qk_copy(6)
            unit_hi(CONV + 1, 0, 3)
            qk_copy(7)
            for m in range(KW):
                if m == 0:
                    act.wait_ge(qk_turned, 2 * NT)
                c_copy(m)
                if m < 2:
                    unit_hi(CONV + m + 2, 0, 3)
                elif m == 2:
                    unit_hi(OUT, 0, 4)

            for i in range(UNITS + 2):
                if i < UNITS:
                    act.wait_ge(neg_ready, i + 1)
                    for h in range(2):
                        s = scores[i % 3][:, h, :]
                        c = 2 * i + h
                        act.activation(s, s, ACT.Exp, bias=neg_max[:, c:c + 1],
                                       accum_out=row_sum[:, c:c + 1]).then_inc(exp_done, 1)
                if i >= 2:
                    u = i - 2
                    act.wait_ge(prob_turned, u + 1)
                    act.activation(probT[u % 2].rearrange("p (b c) -> p b c", b=2), bank[:, 4:6, :],
                                   ACT.Copy).then_inc(probT_ready, 1)
                if 2 <= i < 2 + KW:
                    m = i - 2
                    act.activation(yc_hi[:, m, :], yT_conv[:, m, :], ACT.Copy,
                                   scale=columns[:, 12 + m:13 + m]).then_inc(yc_hi_ready, 1)
                if 2 + KW <= i < 6 + KW:
                    unit_hi(OUT + 1, i - 2 - KW, i - 1 - KW)
            act.dma_start(x_sb, x_d[0].rearrange("(t p) d -> p t d", p=P)).then_inc(x_reloaded, 16)
            act.dma_start(g_ffn, g_ffn_d[0].partition_broadcast(P)).then_inc(g_ffn_loaded, 16)
            for m in range(KW):
                act.wait_ge(y_attn_ready, NT * (m + 1))
                act.activation(ya_hi[:, m, :], yT_attn[:, m, :], ACT.Copy,
                               scale=columns[:, 16 + m:17 + m]).then_inc(ya_hi_ready, 1)
            root(2 * NT)

            def x2_half(t):
                act.wait_ge(x2_turned, 2 * t + 1)
                act.activation(x2T[t % 2][:, 0:512], bank[:, 4 + 2 * (t % 2), :], ACT.Copy).then_inc(x2T_ready, 1)

            for t in range(NT):
                if t:
                    x2_half(t - 1)
                act.wait_ge(mix_added, 2 * NT + 2 * t + 2)
                act.activation(h2[:, t, :], x_sb[:, t, :], ACT.Square,
                               accum_out=sums[:, NT + t:NT + t + 1]).then_inc(squared, 1)
                if t == NT - 1:
                    x2_half(t)
                root(1)
            act.dma_start(g_final, g_final_d.partition_broadcast(P)).then_inc(g_final_loaded, 16)
            act.wait_ge(shifted_ready, 1)
            act.activation(aff[:, :, :], aff[:, :, :], ACT.Exp).then_inc(aff_exp, 1)

            with act.Fori(0, PAIRS) as pair:
                act.wait_ge(gathered, pair * 2 + 1)
                act.activation(xeT[:, 0:4, :], bank[:, 6, :].rearrange("p (k s) -> p k s", k=4),
                               ACT.Copy).then_inc(xeT_ready, 1)
                for j in range(2):
                    for r in range(ROUNDS):
                        n = 2 * j + r
                        act.wait_ge(slots_used, pair * PAIR_SLOTS
                                    + (FRONT_USES + EXPERT_SLOTS * j + ROUND_SLOTS * (r + 1)))
                        act.wait_ge(hid_ready, pair * 4 + (n + 1))
                        act.activation(silu[r], bank[:, r, :], ACT.Silu).then_inc(silu_ready, 1)
                    for r in range(ROUNDS):
                        act.wait_ge(hid_turned, pair * 4 + (2 * j + r + 1))
                        dst = hidT[:, 8 * r:8 * r + 8, :].rearrange("p (c b) s -> p b c s", c=2)
                        src = bank[:, 5, :].rearrange("p (b c s) -> p b c s", b=4, c=2)
                        act.activation(dst, src, ACT.Copy).then_inc(hidT_ready, 1)
                    act.wait_ge(slots_used, pair * PAIR_SLOTS + (FRONT_USES + EXPERT_SLOTS * (j + 1)))
                    act.activation(y_pair[CAP * j:CAP * j + CAP, 0:512], bank[0:64, 4, :],
                                   ACT.Copy).then_inc(y_ready, 1)

            for t in range(NT):
                act.wait_ge(x_added, 2 * NT * (PAIRS - 1) + 2 * t + 2)
                act.activation(ring_flat[:, D * t:D * t + D], x_sb[:, t, :], ACT.Square,
                               accum_out=sums[:, 2 * NT + t:2 * NT + t + 1]).then_inc(squared, 1)
                root(1)

        @block.vector
        def _(dve):
            steps = [0]
            norms = [0]

            def step(ins):
                steps[0] += 1
                ins.then_inc(dve_step, 1)
                dve.wait_ge(dve_step, steps[0])

            def inverse_root(totals, count, width, out=None):
                n = norms[0]
                norms[0] += 1
                var, rt, inv, tmp = (norm[:, n % 4, i, 0:width * len(totals)] for i in range(4))
                for i, total in enumerate(totals):
                    ins = dve.tensor_scalar(var[:, width * i:width * i + width], total, 1.0 / count, RMS_EPS,
                                            ALU.mult, ALU.add)
                ins.then_inc(var_ready, 1)
                dve.wait_ge(root_ready, n + 1)
                step(dve.reciprocal(inv, rt))
                step(dve.tensor_tensor(tmp, inv, inv, ALU.mult))
                step(dve.tensor_tensor(tmp, tmp, var, ALU.mult))
                step(dve.tensor_scalar(tmp, tmp, -0.5, 1.5, ALU.mult, ALU.add))
                out = inv if out is None else out
                step(dve.tensor_tensor(out, inv, tmp, ALU.mult))
                return out

            def first_norm(t):
                dve.wait_ge(squared, t + 1)
                inv = inverse_root([sums[:, t:t + 1]], D, 1)
                dve.tensor_scalar(xn[:, t, :], x_sb[:, t, :], inv, None, ALU.mult).then_inc(xn_ready, 1)

            def hT_lo_make(t):
                for i in range(2):
                    dve.wait_ge(hT_hi_ready, 2 * t + i + 1)
                    for k in range(4 * i, 4 * i + 4):
                        ins = dve.scalar_tensor_tensor(out=hT_lo[:, k, P * t:P * t + P], in0=turned_h(t, k),
                                                       scalar=mix_gains[:, k:k + 1],
                                                       in1=hT_hi[:, k, P * t:P * t + P].bitcast(F32),
                                                       op0=ALU.mult, op1=ALU.subtract)
                    ins.then_inc(hT_lo_ready, 1)

            def unit_lo(u, c0, c1):
                for c in range(c0, c1):
                    dve.wait_ge(hi_ready, pieces_before(u) + c + 1)
                    dve.tensor_tensor(unit_piece(u, c, w_lo), unit_piece(u, c, lo_raw),
                                      unit_piece(u, c, w_hi).bitcast(F32), ALU.subtract).then_inc(lo_ready, 1)

            first_norm(0)
            dve.wait_ge(mix_gains_turned, 1)
            dve.tensor_copy(mix_gains[:, :], bank[:, 3, 0:KD]).then_inc(mix_gains_ready, 1)
            first_norm(1)
            dve.wait_ge(mix_gains_ready, 1)
            hT_lo_make(0)
            unit_lo(V, 0, 2)
            hT_lo_make(1)
            unit_lo(V, 2, 4)
            first_norm(2)
            hT_lo_make(2)
            first_norm(3)
            hT_lo_make(3)
            dve.wait_ge(rows_loaded, 80)
            dve.tensor_copy(pos_rows, pos_int.bitcast(I32)).then_inc(pos_ready, 1)
            unit_lo(Q, 0, 4)
            dve.wait_ge(rows_turned, 2)
            dve.tensor_copy(columns[:, :], bank[:, 3, 8:40]).then_inc(columns_ready, 1)

            dve.wait_ge(consts_ready, 13)
            dve.wait_ge(columns_ready, 1)
            ang = angles[:, :].rearrange("p (t i) -> p t i", t=NT)
            step(dve.tensor_tensor(ang, columns[:, 28:32].unsqueeze(2).to_broadcast([P, NT, ROT_HALF]),
                                   inv_freq[:, :].unsqueeze(1).to_broadcast([P, NT, ROT_HALF]), ALU.mult))
            half = NT * ROT_HALF
            for i in range(2):
                step(dve.tensor_scalar(turns[:, half * i:half * i + half], angles[:, :],
                                       1.0 / (2.0 * math.pi), 0.25 * i, ALU.mult, ALU.add))
            step(dve.tensor_scalar(turns[:, :], turns[:, :], ROUND, None, ALU.add))
            step(dve.tensor_scalar(turns[:, :], turns[:, :], ROUND, None, ALU.subtract))
            for i in range(2):
                dst = reduced[:, half * i:half * i + half]
                src = angles[:, :]
                for part in TURN_PARTS:
                    step(dve.scalar_tensor_tensor(out=dst, in0=turns[:, half * i:half * i + half], scalar=-part,
                                                  in1=src, op0=ALU.mult, op1=ALU.add))
                    src = dst
            step(dve.tensor_scalar(reduced[:, half:2 * half], reduced[:, half:2 * half], math.pi / 2, None, ALU.add))
            dve.tensor_scalar(reduced[:, :], reduced[:, :], PI_INSIDE, -PI_INSIDE,
                              ALU.min, ALU.max).then_inc(turns_ready, 1)

            dist_i, a_i = dist.bitcast(I32), mask_a.bitcast(I32)
            reach = [float((window // 2 // dil * dil) ** 2) for window, dil in PATTERNS]

            def strip_start():
                step(dve.tensor_tensor(mask_b, dist_i, dist_i, ALU.mult))
                step(dve.tensor_scalar(strip[:, :], mask_b, reach[0], None, ALU.is_le))

            def strip_add(i):
                for (window, dil), far in [(PATTERNS[i], reach[i])]:
                    step(dve.tensor_scalar(a_i, dist_i, dil - 1, None, ALU.bitwise_and))
                    step(dve.tensor_scalar(mask_a, a_i, 0.0, None, ALU.is_equal))
                    step(dve.scalar_tensor_tensor(out=mask_a, in0=mask_b, scalar=far, in1=mask_a,
                                                  op0=ALU.is_le, op1=ALU.mult))
                    step(dve.tensor_tensor(strip[:, :], strip[:, :], mask_a, ALU.add))

            def strip_end():
                step(dve.tensor_scalar(mask_a, strip[:, :], 2.0, math.log(2.0), ALU.is_equal, ALU.mult))
                step(dve.tensor_scalar(mask_b, strip[:, :], 3.0, math.log(3.0), ALU.is_equal, ALU.mult))
                step(dve.tensor_tensor(mask_a, mask_a, mask_b, ALU.add))
                step(dve.tensor_scalar(strip[:, :], strip[:, :], 0.0, MASKED, ALU.is_equal, ALU.mult))
                dve.tensor_tensor(strip[:, :], strip[:, :], mask_a, ALU.add).then_inc(strip_ready, 1)

            def rope(j):
                t = j % NT
                heads = stage[j % STAGES].rearrange("p (h c) -> p h c", c=HEAD_DIM)
                first, second = heads[:, :, 0:ROT_HALF], heads[:, :, ROT_HALF:2 * ROT_HALF]
                sin, cos = (sin_cos[:, half * i + ROT_HALF * t:half * i + ROT_HALF * t + ROT_HALF]
                            .unsqueeze(1).to_broadcast([P, NH, ROT_HALF]) for i in range(2))
                dve.wait_ge(item_copied, NT + j + 1)
                if j:
                    dve.wait_ge(rope_done, 2 * j)
                step(dve.tensor_tensor(rot[:, 0], first, cos, ALU.mult))
                step(dve.tensor_tensor(rot[:, 1], second, sin, ALU.mult))
                step(dve.tensor_tensor(rot[:, 2], second, cos, ALU.mult))
                step(dve.tensor_tensor(rot[:, 3], first, sin, ALU.mult))
                dve.tensor_tensor(first, rot[:, 0], rot[:, 1], ALU.subtract).then_inc(rope_done, 1)
                dve.tensor_tensor(second, rot[:, 2], rot[:, 3], ALU.add).then_inc(rope_done, 1)

            def kT_copy(t):
                dve.wait_ge(qk_turned, NT + t + 1)
                if t == 0:
                    dve.wait_ge(kT_zeroed, 2)
                for h in range(2):
                    half_rows = slice(HEAD_DIM * h, HEAD_DIM * h + HEAD_DIM)
                    dve.tensor_copy(kT[half_rows, h, :, P * t:P * t + P],
                                    bank[half_rows, 6 + t % 2, :].rearrange("p (m s) -> p m s", m=KW)).then_inc(kT_ready, 1)

            def conv(m):
                base = conv_bank(m)
                z = z_buf[m % 2]
                y = yT_conv[:, m, :]
                tap = [columns[:, KW * i + m:KW * i + m + 1] for i in range(TAPS)]
                dve.wait_ge(c_copied, m + 1)
                if m < 2:
                    step(dve.memset(z[:, 0:1], 0.0))
                    step(dve.memset(z[:, S + 1:S + 2], 0.0))
                dve.wait_ge(conv_done, 3 * m + 2)
                step(dve.tensor_tensor(z[:, 1:S + 1], c_buf[m % 2], bank[:, base + 1, :], ALU.mult))
                step(dve.tensor_scalar(y, z[:, 0:S], tap[0], None, ALU.mult))
                step(dve.scalar_tensor_tensor(out=y, in0=z[:, 1:S + 1], scalar=tap[1], in1=y,
                                              op0=ALU.mult, op1=ALU.add))
                step(dve.scalar_tensor_tensor(out=y, in0=z[:, 2:S + 2], scalar=tap[2], in1=y,
                                              op0=ALU.mult, op1=ALU.add))
                dve.wait_ge(conv_done, 3 * m + 3)
                dve.tensor_tensor(y, y, bank[:, base + 2, :], ALU.mult).then_inc(y_conv_ready, 1)

            dve.wait_ge(sin_ready, 1)
            rope(0)
            unit_lo(K, 0, 2)
            rope(1)
            unit_lo(K, 2, 4)
            strip_start()
            rope(2)
            strip_add(1)
            rope(3)
            unit_lo(CONV, 0, 3)
            rope(4)
            strip_add(2)
            rope(5)
            kT_copy(0)
            strip_end()
            rope(6)
            kT_copy(1)
            unit_lo(CONV + 1, 0, 3)
            rope(7)
            dve.wait_ge(rope_done, 4 * NT)
            kT_copy(2)
            kT_copy(3)
            for m in range(KW):
                conv(m)
                if m < 2:
                    unit_lo(CONV + m + 2, 0, 3)
            dve.wait_ge(router_loaded, 16)
            dve.tensor_tensor(router[:, :].rearrange("p (k e) -> p k e", k=KD),
                              router[:, :].rearrange("p (k e) -> p k e", k=KD),
                              columns[:, 20:28].unsqueeze(2).to_broadcast([P, KD, E]),
                              ALU.mult).then_inc(router_scaled, 1)

            def take_y(u):
                m, t = divmod(u, NT)
                dve.wait_ge(pv_done, u + 1)
                dve.tensor_copy(yT_attn[:, m, P * t:P * t + P], bank[:, 6 + u % 2, 0:P]).then_inc(y_attn_ready, 1)

            for i in range(UNITS + 1):
                if i < UNITS:
                    t = i % NT
                    seen = strip[:, S - P - P * t:2 * S - P - P * t]
                    for h in range(2):
                        c = 2 * i + h
                        dve.wait_ge(scores_done, c + 1)
                        dve.tensor_tensor_reduce(out=scores[i % 3][:, h, :], in0=bank[:, 2 * (i % 2) + h, :],
                                                 in1=seen, scale=1.0, scalar=-3e38, op0=ALU.add, op1=ALU.max,
                                                 accum_out=row_max[:, c:c + 1]).then_inc(max_ready, 1)
                    dve.wait_ge(max_ready, 2 * i + 2)
                    dve.tensor_scalar(neg_max[:, 2 * i:2 * i + 2], row_max[:, 2 * i:2 * i + 2], -1.0, None,
                                      ALU.mult).then_inc(neg_ready, 1)
                if i >= 1:
                    u = i - 1
                    dve.wait_ge(exp_done, 2 * u + 2)
                    dve.reciprocal(row_inv[:, 2 * u:2 * u + 2], row_sum[:, 2 * u:2 * u + 2]).then_inc(inv_ready, 1)
                    dve.wait_ge(inv_ready, u + 1)
                    for h in range(2):
                        s = scores[u % 3][:, h, :]
                        dve.tensor_scalar(s, s, row_inv[:, 2 * u + h:2 * u + h + 1], None,
                                          ALU.mult).then_inc(prob_ready, 1)
                if i >= 3:
                    take_y(i - 3)
                if 3 <= i < 3 + KW:
                    m = i - 3
                    dve.wait_ge(yc_hi_ready, m + 1)
                    dve.scalar_tensor_tensor(out=yc_lo[:, m, :], in0=yT_conv[:, m, :],
                                             scalar=columns[:, 12 + m:13 + m], in1=yc_hi[:, m, :].bitcast(F32),
                                             op0=ALU.mult, op1=ALU.subtract).then_inc(yc_lo_ready, 1)
            take_y(UNITS - 2)
            take_y(UNITS - 1)

            def add_mix(o, inv):
                t, n = divmod(o % (2 * NT), 2)
                xs = x_sb[:, t, B * n:B * n + B]
                dve.wait_ge(mix_done, o + 1)
                if o >= 2 * NT:
                    dve.wait_ge(mix_added, o - 2 * NT + 1)
                dve.scalar_tensor_tensor(out=xs, in0=bank[:, o % 3, :], scalar=inv[:, t:t + 1], in1=xs,
                                         op0=ALU.mult, op1=ALU.add).then_inc(mix_added, 1)

            for m in range(KW):
                dve.wait_ge(ya_hi_ready, m + 1)
                dve.scalar_tensor_tensor(out=ya_lo[:, m, :], in0=yT_attn[:, m, :],
                                         scalar=columns[:, 16 + m:17 + m], in1=ya_hi[:, m, :].bitcast(F32),
                                         op0=ALU.mult, op1=ALU.subtract).then_inc(ya_lo_ready, 1)
            dve.wait_ge(attn_sums_done, NT)
            inverses = inverse_root([bank[:, 7, P:P + 96 * NT:96], bank[:, 3, 0:96 * NT:96]], W, NT)
            inv_conv, inv_attn = inverses[:, 0:NT], inverses[:, NT:2 * NT]
            dve.wait_ge(x_reloaded, 16)
            for o in range(2 * NT):
                add_mix(o, inv_conv)
            dve.wait_ge(g_ffn_loaded, 16)

            def x2_half(t):
                dve.wait_ge(x2_turned, 2 * t + 2)
                dve.tensor_copy(x2T[t % 2][:, 512:1024], bank[:, 5 + 2 * (t % 2), :]).then_inc(x2T_ready, 1)

            for t in range(NT):
                add_mix(2 * NT + 2 * t, inv_attn)
                add_mix(2 * NT + 2 * t + 1, inv_attn)
                if t:
                    x2_half(t - 1)
                if t == NT - 1:
                    x2_half(t)
                dve.wait_ge(squared, NT + t + 1)
                inv = inverse_root([sums[:, NT + t:NT + t + 1]], D, 1, out=small[:, 3, t:t + 1])
                dve.scalar_tensor_tensor(out=h2[:, t, :], in0=x_sb[:, t, :], scalar=inv, in1=g_ffn,
                                         op0=ALU.mult, op1=ALU.mult).then_inc(h2_ready, 1)

            products = bank[:, 3, 0:96 * NT].rearrange("p (t c) -> p t c", t=NT)[:, :, 0:E]
            dve.wait_ge(logits_done, NT)
            step(dve.tensor_tensor(aff[:, :, :], products, small[:, 3, :].unsqueeze(2).to_broadcast([P, NT, E]),
                                   ALU.mult))
            step(dve.tensor_reduce(small[:, 0, :], aff[:, :, :], AX.X, ALU.max))
            dve.tensor_tensor(aff[:, :, :], aff[:, :, :], small[:, 0, :].unsqueeze(2).to_broadcast([P, NT, E]),
                              ALU.subtract).then_inc(shifted_ready, 1)
            dve.wait_ge(aff_exp, 1)
            step(dve.tensor_reduce(small[:, 1, :], aff[:, :, :], AX.X, ALU.add))
            step(dve.reciprocal(small[:, 2, :], small[:, 1, :]))
            dve.tensor_tensor(aff[:, :, :], aff[:, :, :], small[:, 2, :].unsqueeze(2).to_broadcast([P, NT, E]),
                              ALU.mult).then_inc(aff_ready, 1)

            dve.wait_ge(aff_turned, NT)
            step(dve.tensor_copy(top_row[0], bank[0:E, 4, :]))
            for i in range(CAP // 8):
                step(dve.max(top8[:, :], top_row[i % 2]))
                step(dve.match_replace(out=top_row[(i + 1) % 2], in_to_replace=top8[:, :],
                                       in_values=top_row[i % 2], imm_value=-1.0))
            taken, other, chosen = top_row[(CAP // 8) % 2], top_row[(CAP // 8 + 1) % 2], top_row[2]
            step(dve.tensor_scalar(chosen, taken, -1.0, None, ALU.is_equal))
            step(dve.memset(other, 1.0))
            step(dve.tensor_tensor_scan(taken, other, chosen, 0.0, ALU.mult, ALU.add))
            dve.tensor_tensor(other, taken, chosen, ALU.mult).then_inc(slot_row_ready, 1)
            dve.wait_ge(slot_row_turned, NT)
            step(dve.tensor_copy(slot_of[:, :, :], bank[:, 5, 0:NT * E].rearrange("p (t e) -> p t e", t=NT)))
            dve.sem_inc(hid_ready, 2)

            with dve.Fori(0, PAIRS) as pair:
                places = slot_of[:, :, bass.ds(pair * 2, 2)]
                gates = aff[:, :, bass.ds(pair * 2, 2)]
                dve.tensor_tensor(picks, slot_ids[:, :].unsqueeze(1).unsqueeze(1).to_broadcast([P, NT, 2, CAP]),
                                  places.unsqueeze(3).to_broadcast([P, NT, 2, CAP]),
                                  ALU.is_equal).then_inc(picks_ready, 1)
                dve.wait_ge(picks_ready, pair + 1)
                dve.tensor_tensor(gated, picks, gates.unsqueeze(3).to_broadcast([P, NT, 2, CAP]),
                                  ALU.mult).then_inc(gated_ready, 1)
                dve.wait_ge(gathered, pair * 2 + 2)
                dve.tensor_copy(xeT[:, 4:8, :], bank[:, 7, :].rearrange("p (k s) -> p k s", k=4)).then_inc(xeT_ready, 1)
                dve.wait_ge(gated_turned, pair + 1)
                dve.tensor_copy(putT, bank[:, 5, :]).then_inc(putT_ready, 1)
                for j in range(2):
                    for r in range(ROUNDS):
                        dve.wait_ge(silu_ready, pair * 4 + (2 * j + r + 1))
                        dve.tensor_tensor(hid[r], silu[r], bank[:, 2 + r, :], ALU.mult).then_inc(hid_ready, 1)
                    dve.wait_ge(slots_used, pair * PAIR_SLOTS + (FRONT_USES + EXPERT_SLOTS * (j + 1)))
                    dve.tensor_copy(y_pair[CAP * j:CAP * j + CAP, 512:1024], bank[64:128, 4, :]).then_inc(y_ready, 1)
                for o in range(2 * NT):
                    t, n = divmod(o, 2)
                    xs = x_sb[:, t, B * n:B * n + B]
                    dve.wait_ge(put_done, pair * (2 * NT) + (o + 1))
                    dve.tensor_tensor(xs, xs, bank[:, 6 + n, :], ALU.add).then_inc(x_added, 1)

            for t in range(NT):
                dve.wait_ge(squared, 2 * NT + t + 1)
                inv = inverse_root([sums[:, 2 * NT + t:2 * NT + t + 1]], D, 1)
                dve.wait_ge(gained, t + 1)
                dve.tensor_scalar(h2[:, t, :], h2[:, t, :], inv, None, ALU.mult).then_inc(final_ready, 1)

        @block.tensor
        def _(pe):
            pe.wait_ge(consts_ready, 2)
            pe.wait_ge(g_mix_loaded, 16)
            pe.transpose(bank[:, 3, 0:KD], mix_rows, ident[0:KD, 0:KD]).then_inc(mix_gains_turned, 1)

            def h_turn(t):
                pe.wait_ge(xn_ready, t + 1)
                if t >= 2:
                    pe.wait_ge(hT_lo_ready, 2 * t - 2)
                for k in range(KD):
                    mm = pe.transpose(turned_h(t, k), xn[:, t, P * k:P * k + P], ident[:, :])
                    if k % 4 == 3:
                        mm.then_inc(xn_turned, 1)

            def rows_turn():
                pe.wait_ge(mix_gains_ready, 1)
                pe.wait_ge(rows_loaded, 80)
                pe.transpose(bank[:, 3, 8:36], gain_rows, ident[0:28, 0:28]).then_inc(rows_turned, 1)
                pe.wait_ge(pos_ready, 1)
                pe.transpose(bank[:, 3, 36:40], pos_rows, ident[0:NT, 0:NT]).then_inc(rows_turned, 1)

            def qkv(n):
                u, t = divmod(n, NT)
                if u == 0:
                    pe.wait_ge(hT_lo_ready, 2 * t + 2)
                if n >= 3:
                    pe.wait_ge(item_copied, n - 2)
                for k in range(KD):
                    if t == 0 and k % 2 == 0:
                        pe.wait_ge(lo_ready, pieces_before(u) + k // 2 + 1)
                    h_hi, h_lo = (part[:, k, P * t:P * t + P] for part in (hT_hi, hT_lo))
                    out = bank[:, n % 3, :]
                    pe.matmul(out, h_hi, unit_k(u, k, w_hi), start=(k == 0), stop=False)
                    pe.matmul(out, h_hi, unit_k(u, k, w_lo), start=False, stop=False)
                    mm = pe.matmul(out, h_lo, unit_k(u, k, w_hi), start=False, stop=(k == KD - 1))
                mm.then_inc(qkv_done, 1)

            def qk_turn(j):
                pe.wait_ge(rope_done, 2 * j + 2)
                if j >= 2:
                    if j - 2 < NT:
                        pe.wait_ge(qT_ready, j - 1)
                    else:
                        pe.wait_ge(kT_ready, 2 * (j - 1 - NT))
                for m in range(KW):
                    mm = pe.transpose(bank[:, 6 + j % 2, P * m:P * m + P],
                                      stage[j % STAGES][:, P * m:P * m + P], ident[:, :])
                mm.then_inc(qk_turned, 1)

            def conv_in(m, i):
                u = CONV + m
                pe.wait_ge(lo_ready, pieces_before(u) + i + 1)
                if i == 0:
                    if m == 0:
                        pe.wait_ge(columns_ready, 1)
                    elif m == 1:
                        pe.wait_ge(item_copied, 3 * NT)
                    else:
                        pe.wait_ge(y_conv_ready, m - 1)
                hi, lo = (unit_piece(u, i, place).rearrange("p (k c) -> p k c", k=KD) for place in (w_hi, w_lo))
                out = bank[:, conv_bank(m) + i, :]
                for k in range(KD):
                    pe.matmul(out, hi[:, k, :], hT_hi[:, k, :], start=(k == 0), stop=False)
                    pe.matmul(out, hi[:, k, :], hT_lo[:, k, :], start=False, stop=False)
                    mm = pe.matmul(out, lo[:, k, :], hT_hi[:, k, :], start=False, stop=(k == KD - 1))
                mm.then_inc(conv_done, 1)

            h_turn(0)
            h_turn(1)
            qkv(0)
            h_turn(2)
            qkv(1)
            h_turn(3)
            qkv(2)
            rows_turn()
            qkv(3)
            qkv(4)
            for j in range(7):
                qkv(5 + j)
                qk_turn(j)
            conv_in(0, 0)
            qk_turn(7)
            for n in range(1, 3 * KW):
                conv_in(n // 3, n % 3)

            def unit_scores(u):
                m, t = divmod(u, NT)
                if u >= 2:
                    pe.wait_ge(max_ready, 2 * u - 2)
                for h in range(2):
                    mm = pe.matmul(bank[:, 2 * (u % 2) + h, :], qT[:, m, P * t:P * t + P], kT[:, h, m, :],
                                   start=True, stop=True)
                    mm.then_inc(scores_done, 1)

            pe.wait_ge(qT_ready, NT)
            pe.wait_ge(kT_ready, 2 * NT)
            pe.wait_ge(y_conv_ready, KW)
            for u in range(3):
                unit_scores(u)
                if u == 0:
                    pe.wait_ge(strip_ready, 1)
            for u in range(UNITS):
                m = u // NT
                pe.wait_ge(prob_ready, 2 * u + 2)
                if u:
                    pe.wait_ge(probT_ready, u)
                for h in range(2):
                    for k in range(NT):
                        mm = pe.transpose(bank[:, 4 + h, P * k:P * k + P],
                                          scores[u % 3][:, h, P * k:P * k + P], ident[:, :])
                        if (u, h, k) == (0, 0, 0):
                            mm.then_inc(slots_used, 6)
                mm.then_inc(prob_turned, 1)
                if u + 3 < UNITS:
                    unit_scores(u + 3)
                pe.wait_ge(probT_ready, u + 1)
                if u >= 2:
                    pe.wait_ge(y_attn_ready, u - 1)
                if u == 3:
                    pe.wait_ge(conv_sq_ready, 1)
                    for s in range(NT):
                        mm = pe.matmul(bank[:, 7, P + 96 * s:P + 96 * s + 96], conv_sq[:, P * s:P * s + P],
                                       ones[:, :].to_broadcast([P, 96]), start=True, stop=True)
                for k in range(NT):
                    for h in range(2):
                        head = 2 * m + h
                        mm = pe.matmul(bank[HEAD_DIM * h:HEAD_DIM * h + HEAD_DIM, 6 + u % 2, 0:P],
                                       v_sb[:, k, HEAD_DIM * head:HEAD_DIM * head + HEAD_DIM],
                                       probT[u % 2][:, 512 * h + P * k:512 * h + P * k + P],
                                       start=(k == 0), stop=(k == NT - 1))
                mm.then_inc(pv_done, 1)

            def mix_group(o):
                g, (t, n) = o // (2 * NT), divmod(o % (2 * NT), 2)
                if o >= 3:
                    pe.wait_ge(mix_added, o - 2)
                u = OUT + g
                y_hi, y_lo = ((yc_hi, yc_lo), (ya_hi, ya_lo))[g]
                for m in range(KW):
                    if o in (0, 2 * NT):
                        pe.wait_ge(out_lo_ready, KW * g + m + 1)
                        pe.wait_ge((yc_lo_ready, ya_lo_ready)[g], m + 1)
                    hi, lo = (unit_piece(u, m, place)[:, B * n:B * n + B] for place in (w_hi, w_lo))
                    tokens = slice(P * t, P * t + P)
                    out = bank[:, o % 3, :]
                    mm = pe.matmul(out, y_hi[:, m, tokens], hi, start=(m == 0), stop=False)
                    if o == 2 * NT and m == 0:
                        mm.then_inc(slots_used, 6)
                    pe.matmul(out, y_hi[:, m, tokens], lo, start=False, stop=False)
                    mm = pe.matmul(out, y_lo[:, m, tokens], hi, start=False, stop=(m == KW - 1))
                mm.then_inc(mix_done, 1)

            def x2_turn(t):
                pe.wait_ge(mix_added, 2 * NT + 2 * t + 2)
                for k in range(KD):
                    mm = pe.transpose(bank[:, 4 + 2 * (t % 2) + k // 4, P * (k % 4):P * (k % 4) + P],
                                      x_sb[:, t, P * k:P * k + P], ident[:, :])
                    if t == NT - 1 and k == 0:
                        mm.then_inc(slots_used, 4)
                    if k % 4 == 3:
                        mm.then_inc(x2_turned, 1)

            def route(t):
                pe.wait_ge(x2T_ready, 2 * t + 2)
                for k in range(KD):
                    mm = pe.matmul(bank[:, 3, 96 * t:96 * t + 96], x2T[t % 2][:, P * k:P * k + P],
                                   router_wide[:, E * k:E * k + 96], start=(k == 0), stop=(k == KD - 1))
                mm.then_inc(logits_done, 1)

            pe.wait_ge(max_ready, 2 * UNITS)
            for o in range(2 * NT):
                if o == 3:
                    pe.wait_ge(attn_sq_ready, 1)
                    for s in range(NT):
                        mm = pe.matmul(bank[:, 3, 96 * s:96 * s + 96], attn_sq[:, P * s:P * s + P],
                                       ones[:, :].to_broadcast([P, 96]), start=True, stop=True)
                        mm.then_inc(attn_sums_done, 1)
                mix_group(o)
            pe.wait_ge(router_scaled, 1)
            pe.wait_ge(var_ready, NT + 1)
            for t in range(NT):
                mix_group(2 * NT + 2 * t)
                mix_group(2 * NT + 2 * t + 1)
                if t:
                    x2_turn(t - 1)
                    route(t - 1)
            x2_turn(NT - 1)
            route(NT - 1)

            pe.wait_ge(aff_ready, 1)
            for t in range(NT):
                pe.transpose(bank[0:E, 4, P * t:P * t + P], aff[:, t, :], ident[:, :]).then_inc(aff_turned, 1)
            pe.wait_ge(slot_row_ready, 1)
            place_row = top_row[(CAP // 8 + 1) % 2]
            for t in range(NT):
                pe.transpose(bank[:, 5, E * t:E * t + E], place_row[:, P * t:P * t + P],
                             ident[0:E, 0:E]).then_inc(slot_row_turned, 1)

            with pe.Fori(0, PAIRS) as pair:
                pe.wait_ge(picks_ready, pair + 1)
                for k in range(KD):
                    for t in range(NT):
                        mm = pe.matmul(bank[:, 6 + k // 4, P * (k % 4):P * (k % 4) + P],
                                       h2[:, t, P * k:P * k + P], picks[:, t, :, :].rearrange("p j s -> p (j s)"),
                                       start=(t == 0), stop=(t == NT - 1))
                    if k % 4 == 3:
                        mm.then_inc(gathered, 1)
                pe.wait_ge(xeT_ready, pair * 2 + 2)
                for j in range(2):
                    tokens = slice(CAP * j, CAP * j + CAP)
                    for r in range(ROUNDS):
                        pe.wait_ge(hid_ready, pair * 4 + (2 * j + r + 1))
                        for q in range(ROUND_SLOTS):
                            i = EXPERT_SLOTS * j + ROUND_SLOTS * r + q
                            pe.wait_ge(slot_loaded[i % RING], pair * (16 * PAIR_SLOTS // RING) + 16 * (i // RING + 1))
                            for kk in range(2):
                                k = 2 * (q // 2) + kk
                                for c in range(2):
                                    mm = pe.matmul(bank[64 * c:64 * c + 64, 2 * (q % 2) + r, :], xeT[:, k, tokens],
                                                   slot_rows(i)[:, kk, B * c:B * c + B],
                                                   start=(k == 0), stop=(k == KD - 1))
                            mm.then_inc(slots_used, 1)
                    if j == 0:
                        pe.wait_ge(gated_ready, pair + 1)
                        for t in range(NT):
                            mm = pe.transpose(bank[:, 5, P * t:P * t + P],
                                              gated[:, t, :, :].rearrange("p j s -> p (j s)"), ident[:, :])
                        mm.then_inc(gated_turned, 1)
                    for r in range(ROUNDS):
                        pe.wait_ge(hid_ready, pair * 4 + (2 * j + r + 3))
                        if r == 0 and j == 0:
                            pe.wait_ge(putT_ready, pair + 1)
                        else:
                            pe.wait_ge(hidT_ready, pair * 4 + (2 * j + r))
                        for b in range(4):
                            mm = pe.transpose(bank[:, 5, P * b:P * b + P], hid[r][:, P * b:P * b + P], ident[:, :])
                        mm.then_inc(hid_turned, 1)
                    if j:
                        pe.wait_ge(y_ready, pair * 4 + 2)
                    pe.wait_ge(hidT_ready, pair * 4 + (2 * j + 2))
                    for q in range(F // 256):
                        i = EXPERT_SLOTS * j + ROUNDS * ROUND_SLOTS + q
                        pe.wait_ge(slot_loaded[i % RING], pair * (16 * PAIR_SLOTS // RING) + 16 * (i // RING + 1))
                        for kk in range(2):
                            f = 2 * q + kk
                            for c in range(2):
                                mm = pe.matmul(bank[64 * c:64 * c + 64, 4, :], hidT[:, f, :],
                                               slot_rows(i)[:, kk, B * c:B * c + B],
                                               start=(f == 0), stop=(f == F // P - 1))
                        mm.then_inc(slots_used, 1)
                pe.wait_ge(y_ready, pair * 4 + 4)
                for o in range(2 * NT):
                    t, n = divmod(o, 2)
                    if o >= 2:
                        pe.wait_ge(x_added, pair * (2 * NT) + (o - 1))
                    pe.matmul(bank[:, 6 + n, :], putT[:, P * t:P * t + P], y_pair[:, B * n:B * n + B],
                              start=True, stop=True).then_inc(put_done, 1)
                pe.wait_ge(x_added, (pair + 1) * (2 * NT))


_INS = ["x", "positions", "g_mix", "w_in", "conv_w", "g_conv_out", "g_attn_out", "w_out", "g_ffn", "w_router",
        "w_gate", "w_up", "w_down", "g_final"]


def kernel(**inputs):
    import concourse.bacc as bacc
    from concourse.bass_utils import run_bass_kernel_spmd

    nc = bacc.Bacc("TRN2", target_bir_lowering=False, num_devices=1)
    arrays, args = {}, []
    for name in _INS:
        a = np.ascontiguousarray(inputs[name])
        arrays[f"in_{name}"] = a
        args.append(nc.dram_tensor(f"in_{name}", a.shape, mybir.dt.from_np(a.dtype), kind="ExternalInput").ap())
    out = nc.dram_tensor("out_0", inputs["x"].shape, F32, kind="ExternalOutput").ap()
    hybrid_layer(nc, *args, out)
    r = run_bass_kernel_spmd(nc, [arrays], core_ids=[0])
    return r.results[0]["out_0"]
```

```python
import math
from contextlib import ExitStack

import numpy as np

import concourse.bass as bass
from concourse import mybir

P = 128
F32 = mybir.dt.float32
F32R = mybir.dt.float32r
I32 = mybir.dt.int32
ALU = mybir.AluOpType
ACT = mybir.ActivationFunctionType
AX = mybir.AxisListType

HEAD_DIM = 64
ROT_HALF = HEAD_DIM // 8
ROPE_THETA = 500000.0
RMS_EPS = 1e-6
MASKED = -1e30
CAPACITY_FACTOR = 2
PATTERNS = ((128, 1), (512, 4), (2048, 16))

def turn_parts(bits, count):
    left, parts = 2.0 * math.pi, []
    for _ in range(count):
        unit = 2.0 ** (math.floor(math.log2(left)) + 1 - bits)
        parts.append(math.floor(left / unit) * unit)
        left -= parts[-1]
    return (*parts, left)


TURN_PARTS = turn_parts(10, 3)
ROUND = 12582912.0
PI_INSIDE = 3.1415925


def hybrid_layer(nc, x_d, positions_d, g_mix_d, w_in_d, conv_w_d, g_conv_d, g_attn_d, w_out_d,
                 g_ffn_d, w_router_d, w_gate_d, w_up_d, w_down_d, g_final_d, out_d):
    _, S, D = x_d.shape
    _, E, _, F = w_gate_d.shape
    W = D // 2
    NT = S // P
    KD = D // P
    KW = W // P
    NH = W // HEAD_DIM
    CAP = CAPACITY_FACTOR * S // E
    B = 512
    ROUNDS = F // (2 * B)
    PAIRS = E // 2
    TAPS = conv_w_d.shape[1]
    assert S == B and D == 2 * B and CAP == 64 and NH == 2 * KW and TAPS == 3

    RING = 15
    OWN_BLOCK = {15: 15, 31: 21, 47: 22}
    SLOT = 2048
    FRONT_BLOCKS = 16
    FRONT_USES = 16
    ROUND_SLOTS = 2 * (D // 256)
    EXPERT_SLOTS = ROUNDS * ROUND_SLOTS + F // 256
    PAIR_SLOTS = 2 * EXPERT_SLOTS
    RING_ITEMS = [i for i in range(PAIR_SLOTS) if i not in OWN_BLOCK]
    assert len(RING_ITEMS) % RING == 0
    FIRST_ITEMS = RING_ITEMS[0:RING] + list(OWN_BLOCK)

    PIECE = 1024
    V, Q, K, CONV, OUT = 0, 1, 2, 3, 3 + KW
    PIECES = [4] * CONV + [3] * KW + [4] * 2
    MIX_ORDER = (3, 1, 2, 0)
    UNITS = KW * NT

    with ExitStack() as es:
        def sb(name, shape, dt=F32):
            return es.enter_context(nc.sbuf_tensor(name, shape, dt))

        def sem(name):
            return es.enter_context(nc.semaphore(name))

        ring_base = -(-nc.sbuf_base // 32) * 32
        ring_flat = sb("ring_flat", [P, FRONT_BLOCKS * SLOT])
        desk = sb("desk", [P, 9 * SLOT + 2])

        def block_of(n, count=1):
            if n < FRONT_BLOCKS:
                return ring_flat[:, SLOT * n:SLOT * (n + count)]
            return desk[:, SLOT * (n - FRONT_BLOCKS):SLOT * (n - FRONT_BLOCKS + count)]

        def split_blocks(name, n, count):
            return nc.alloc_sbuf_tensor_at(name, [P, SLOT * count], F32R, offset=ring_base + 4 * SLOT * n)

        PLACES = (0, 8, 12)
        lo_raw = [block_of(b, 2) for b in PLACES]
        unit_split = [split_blocks(f"unit_split{g}", b, 4) for g, b in enumerate(PLACES)]
        w_lo = [split[:, 0:2 * SLOT] for split in unit_split]
        w_hi = [split[:, 2 * SLOT:4 * SLOT] for split in unit_split]
        h_split = split_blocks("h_split", 4, 4)
        hT_hi = h_split[:, 0:2 * SLOT].rearrange("p (k t) -> p k t", k=KD)
        hT_lo = h_split[:, 2 * SLOT:4 * SLOT].rearrange("p (k t) -> p k t", k=KD)
        yc_hi = h_split[:, 2 * SLOT:3 * SLOT].rearrange("p (m t) -> p m t", m=KW)
        yc_lo = h_split[:, 3 * SLOT:4 * SLOT].rearrange("p (m t) -> p m t", m=KW)
        g_final = block_of(0)[:, 0:D]
        r1 = block_of(16)
        mask_b = r1[:, 0:896]
        probT = [r1[:, 1024 * b:1024 * b + 1024] for b in range(2)]
        x2T = probT
        xeT = r1[:, 0:1024].rearrange("p (k s) -> p k s", k=KD)
        hidT = r1[:, 1024:2048].rearrange("p (f s) -> p f s", s=CAP)
        rows = block_of(17)
        gain_rows, mix_rows = rows[0:28, 0:128], rows[0:KD, 128:256]
        pos_int, pos_rows = rows[0:NT, 256:384], rows[0:NT, 384:512]
        yT_conv = rows.rearrange("p (m t) -> p m t", m=KW)
        yT_attn = block_of(18).rearrange("p (m t) -> p m t", m=KW)
        dist, mask_a = block_of(18)[:, 0:896], block_of(18)[:, 896:1792]
        h2 = block_of(17, 2).rearrange("p (t d) -> p t d", t=NT)
        r3 = block_of(19)
        v_sb = r3.rearrange("p (t c) -> p t c", t=NT)
        top_row = [r3[0:E, 512 * b:512 * b + 512] for b in range(3)]
        top_ones = r3[0:E, 1536:2048]
        silu = [r3[:, 512 * b:512 * b + 512] for b in range(2)]
        hid = [r3[:, 1024 + 512 * b:1536 + 512 * b] for b in range(2)]
        r4 = block_of(20)
        qT = r4.rearrange("p (m t) -> p m t", m=KW)
        g_ffn = r4[:, 0:1024]
        attn_sq, attn_sq1 = r4[:, 1024:1536], r4[:, 1536:2048]
        y_pair = r4[:, 0:1024]
        gated = r4[:, 1024:1536].rearrange("p (t j s) -> p t j s", t=NT, j=2)
        putT = r4[:, 1536:2048]
        xn = block_of(21, 2).rearrange("p (t d) -> p t d", t=NT)
        kT = block_of(21, 2).rearrange("p (h m t) -> p h m t", h=2, m=KW)
        ya_split = split_blocks("ya_split", 21, 2)
        ya_hi = ya_split[:, 0:SLOT].rearrange("p (m t) -> p m t", m=KW)
        ya_lo = ya_split[:, SLOT:2 * SLOT].rearrange("p (m t) -> p m t", m=KW)
        SPLIT_FROM = 1
        q_split = split_blocks("q_split", 20, 1)
        score_split = split_blocks("score_split", 0, 3)
        q_lo = q_split[:, :].rearrange("p (m t) -> p m t", m=KW)
        k_lo = ya_split[:, :].rearrange("p (h m t) -> p h m t", h=2, m=KW)
        q_hi = score_split[:, 0:(KW - 1) * S].rearrange("p (m t) -> p m t", m=KW - 1)
        k_hi = score_split[:, (KW - 1) * S:3 * (KW - 1) * S].rearrange("p (h m t) -> p h m t", h=2, m=KW - 1)
        ZW = S + 2
        x_reg = desk[:, 7 * SLOT:9 * SLOT + 2]
        x_sb = x_reg[:, 0:NT * D].rearrange("p (t d) -> p t d", t=NT)
        STAGES = 3
        stage = [x_reg[:, 512 * b:512 * b + 512] for b in range(STAGES)]
        rot = x_reg[:, 2048:2304].rearrange("p (i h c) -> p i h c", i=4, h=NH)
        z_buf = [x_reg[:, b:b + ZW] for b in (2048, 0)]
        c_buf = [x_reg[:, b + ZW:b + ZW + S] for b in (2048, 0)]
        conv_sq, conv_sq1 = x_reg[:, 3074:3586], x_reg[:, 3586:4098]
        scores = [x_reg[:, 1024 * b:1024 * b + 1024].rearrange("p (h k) -> p h k", h=2) for b in range(3)]
        strip = sb("strip", [P, 2 * S - P])
        picks = strip[:, 0:512].rearrange("p (t j s) -> p t j s", t=NT, j=2)
        ident = sb("ident", [P, P])
        ones = sb("ones", [P, 1])
        eps = sb("eps", [P, 1])
        eps_root = sb("eps_root", [P, 1])
        slot_ids = sb("slot_ids", [P, CAP])
        router_wide = sb("router_wide", [P, KD * E + 96 - E])
        router = router_wide[:, 0:KD * E]
        inv_freq = sb("inv_freq", [P, ROT_HALF])
        angles = sb("angles", [P, NT * ROT_HALF])
        turns = sb("turns", [P, 2 * NT * ROT_HALF])
        reduced = sb("reduced", [P, 2 * NT * ROT_HALF])
        sin_cos = sb("sin_cos", [P, 2 * NT * ROT_HALF])
        mix_gains = sb("mix_gains", [P, KD])
        columns = sb("columns", [P, 32])
        sums = sb("sums", [P, 3 * NT])
        norm = sb("norm", [P, 4, 4, 1])
        wide_norm = sb("wide_norm", [P, 2, 4, NT])
        row_max = sb("row_max", [P, 2 * UNITS])
        neg_max = sb("neg_max", [P, 2 * UNITS])
        row_sum = sb("row_sum", [P, 2 * UNITS])
        row_inv = sb("row_inv", [P, 2 * UNITS])
        aff = sb("aff", [P, NT, E])
        slot_of = sb("slot_of", [P, NT, E])
        small = sb("small", [P, 4, NT])
        top8 = sb("top8", [E, 8])
        bank = es.enter_context(nc.psum_tensor("bank", [P, 8, B], F32))

        x_loaded = [sem(f"x_loaded{t}") for t in range(NT)]
        g_mix_loaded = sem("g_mix_loaded")
        rows_loaded = sem("rows_loaded")
        router_loaded = sem("router_loaded")
        router_scaled = sem("router_scaled")
        conv_sums_done = sem("conv_sums_done")
        g_ffn_loaded = sem("g_ffn_loaded")
        g_final_loaded = sem("g_final_loaded")
        unit_loaded = [sem(f"unit{u}_loaded") for u in range(len(PIECES))]
        v_rest_loaded = sem("v_rest_loaded")
        hi_ready = sem("hi_ready")
        lo_ready = sem("lo_ready")
        pool_lo_ready = sem("pool_lo_ready")
        mix_gains_turned = sem("mix_gains_turned")
        mix_gains_ready = sem("mix_gains_ready")
        hT_hi_ready = sem("hT_hi_ready")
        yc_hi_ready = sem("yc_hi_ready")
        ya_hi_ready = sem("ya_hi_ready")
        slot_loaded = {b: sem(f"slot_loaded{b}") for b in (*range(RING), *OWN_BLOCK.values())}
        slots_used = sem("slots_used")
        out_stored = sem("out_stored")
        pool_step = sem("pool_step")
        consts_ready = sem("consts_ready")
        eps_ready = sem("eps_ready")
        table_ready = sem("table_ready")
        pos_ready = sem("pos_ready")
        rows_turned = sem("rows_turned")
        columns_ready = sem("columns_ready")
        dve_step = sem("dve_step")
        squared = sem("squared")
        var_ready = sem("var_ready")
        root_ready = sem("root_ready")
        wide_root_ready = sem("wide_root_ready")
        xn_ready = sem("xn_ready")
        xn_turned = sem("xn_turned")
        hT_lo_ready = sem("hT_lo_ready")
        strip_ready = sem("strip_ready")
        turns_ready = sem("turns_ready")
        sin_ready = sem("sin_ready")
        kT_zeroed = sem("kT_zeroed")
        conv_done = sem("conv_done")
        c_copied = sem("c_copied")
        y_conv_ready = sem("y_conv_ready")
        conv_sq_ready = sem("conv_sq_ready")
        yc_lo_ready = sem("yc_lo_ready")
        qkv_done = sem("qkv_done")
        item_copied = sem("item_copied")
        rope_done = sem("rope_done")
        qk_turned = sem("qk_turned")
        qT_ready = sem("qT_ready")
        kT_ready = sem("kT_ready")
        score_hi_ready = sem("score_hi_ready")
        score_lo_ready = sem("score_lo_ready")
        scores_done = sem("scores_done")
        max_ready = sem("max_ready")
        neg_ready = sem("neg_ready")
        exp_done = sem("exp_done")
        inv_ready = sem("inv_ready")
        prob_ready = sem("prob_ready")
        prob_turned = sem("prob_turned")
        probT_ready = sem("probT_ready")
        pv_done = sem("pv_done")
        y_attn_ready = sem("y_attn_ready")
        attn_sq_ready = sem("attn_sq_ready")
        attn_sums_done = sem("attn_sums_done")
        ya_lo_ready = sem("ya_lo_ready")
        mix_done = sem("mix_done")
        mix_added = sem("mix_added")
        h2_ready = sem("h2_ready")
        x2_turned = sem("x2_turned")
        x2T_ready = sem("x2T_ready")
        logits_done = sem("logits_done")
        shifted_ready = sem("shifted_ready")
        aff_exp = sem("aff_exp")
        aff_ready = sem("aff_ready")
        aff_turned = sem("aff_turned")
        top_ones_ready = sem("top_ones_ready")
        top8_ready = sem("top8_ready")
        slot_row_ready = sem("slot_row_ready")
        slot_row_turned = sem("slot_row_turned")
        picks_ready = sem("picks_ready")
        gated_ready = sem("gated_ready")
        gathered = sem("gathered")
        gated_turned = sem("gated_turned")
        putT_ready = sem("putT_ready")
        xeT_low_ready = sem("xeT_low_ready")
        xeT_high_ready = sem("xeT_high_ready")
        silu_ready = sem("silu_ready")
        hid_ready = sem("hid_ready")
        hid_turned = sem("hid_turned")
        hidT_ready = sem("hidT_ready")
        y_ready = sem("y_ready")
        put_done = sem("put_done")
        x_added = sem("x_added")
        gained = sem("gained")
        inverse_ready = sem("inverse_ready")
        final_left_ready = sem("final_left_ready")
        final_right_ready = sem("final_right_ready")

        def unit_piece(u, c, place):
            return place[u % 3][:, PIECE * c:PIECE * c + PIECE]

        def pieces_before(u):
            return sum(PIECES[:u])

        def lo_wait(u, c):
            if u == V and c % 2 == 0:
                return pool_lo_ready, c // 2 + 1
            if u == Q:
                return pool_lo_ready, 2 + c + 1
            if u >= OUT:
                return pool_lo_ready, 6 + 4 * (u - OUT) + c + 1
            return lo_ready, c // 2 + 1 if u == V else 2 + pieces_before(u) - pieces_before(K) + c + 1

        def unit_k(u, k, place):
            return place[u % 3][:, W * k:W * k + W]

        def item_source(pair, e, i):
            if i < ROUNDS * ROUND_SLOTS:
                r, q = divmod(i, ROUND_SLOTS)
                w = (w_gate_d, w_up_d)[q % 2]
                row = 256 * (q // 2)
                if i + EXPERT_SLOTS * (e % 2) in OWN_BLOCK:
                    src = w[0].rearrange("e d f -> (e d) f")[bass.ds(pair * (2 * D) + (D * e + row), 256),
                                                             1024 * r:1024 * r + 1024]
                else:
                    src = w[0, pair * 2 + e, row:row + 256, 1024 * r:1024 * r + 1024]
            else:
                n, q = divmod(i - ROUNDS * ROUND_SLOTS, F // 512)
                src = w_down_d[0].rearrange("e f d -> (e f) d")[bass.ds(pair * (2 * F) + (F * e + 512 * q), 512),
                                                                 B * n:B * n + B]
            return src.rearrange("(k p) c -> p k c", p=P)

        def item_block(i):
            return OWN_BLOCK[i] if i in OWN_BLOCK else RING_ITEMS.index(i) % RING

        def item_loads(pair, i):
            if i in OWN_BLOCK:
                return pair * 16 + 16
            return pair * (16 * (len(RING_ITEMS) // RING)) + 16 * (RING_ITEMS.index(i) // RING + 1)

        def item_after(i):
            if i in OWN_BLOCK:
                return 1, i
            ahead, r = divmod(RING_ITEMS.index(i) + RING, len(RING_ITEMS))
            return ahead, RING_ITEMS[r]

        def slot_rows(i):
            return block_of(item_block(i)).rearrange("p (k c) -> p k c", k=2)

        def down_rows(i):
            return block_of(item_block(i)).rearrange("p (k c) -> p k c", k=4)

        def down_uses(j, n):
            return FRONT_USES + EXPERT_SLOTS * (j + 1) - (1 - n) * (F // 512)

        def turned_h(t, k):
            return bank[:, 6 - 2 * (t % 2) + k // 4, P * (k % 4):P * (k % 4) + P]

        def mix_place(o):
            g, i = divmod(o, 2 * NT)
            t, n = divmod(i, 2)
            return g, t if g else MIX_ORDER[t], n

        LAST_PUTS = [(0, 0), (0, 1), (0, 2), (1, 0), (1, 1), (1, 2), (0, 3), (1, 3)]
        LAST_ADDS = 2 * NT * (PAIRS - 1)

        def last_add(n, t):
            return LAST_PUTS.index((n, t)) + 1

        def score_bank(u):
            return 2 * (u % 2) if u else 6

        def last_bank(n, t):
            return t if n else 6 + t % 2

        def last_gain(n, t):
            return last_add(n, t)

        def conv_bank(m):
            return 3 - 3 * (m % 2)

        block = es.enter_context(nc.Block())

        @block.sync
        def _(sp):
            def load_x(t):
                sp.dma_start(x_sb[:, t, :], x_d[0, P * t:P * t + P, :]).then_inc(x_loaded[t], 16)

            def load_rows(u, k0, k1, loaded):
                col = (5 * W, 3 * W, 4 * W)[u]
                src = w_in_d[0, P * k0:P * k1, col:col + W].rearrange("(k p) c -> p k c", p=P)
                dst = lo_raw[u % 3][:, W * k0:W * k1].rearrange("p (k c) -> p k c", c=W)
                sp.dma_start(dst, src).then_inc(loaded, 16)

            load_x(0)
            load_rows(V, 0, 4, unit_loaded[V])
            load_x(1)
            load_rows(V, 4, 8, v_rest_loaded)
            load_x(2)
            load_x(3)
            load_rows(Q, 0, 8, unit_loaded[Q])
            sp.dma_start(gain_rows[0:12, :], conv_w_d[0].rearrange("w (c p) -> (w c) p", p=P)).then_inc(rows_loaded, 16)
            sp.dma_start(gain_rows[12:16, :], g_conv_d[0].rearrange("(c p) -> c p", p=P)).then_inc(rows_loaded, 16)
            sp.dma_start(gain_rows[16:20, :], g_attn_d[0].rearrange("(c p) -> c p", p=P)).then_inc(rows_loaded, 16)
            sp.dma_start(gain_rows[20:28, :], g_ffn_d[0].rearrange("(c p) -> c p", p=P)).then_inc(rows_loaded, 16)
            sp.dma_start(pos_int.bitcast(I32), positions_d[0].rearrange("(t p) -> t p", p=P)).then_inc(rows_loaded, 16)
            load_rows(K, 0, 8, unit_loaded[K])
            sp.dma_start(router[:, :].rearrange("p (k e) -> p k e", k=KD),
                         w_router_d[0].rearrange("(k p) e -> p k e", p=P)).then_inc(router_loaded, 16)
            for m in range(KW):
                u = CONV + m
                if m < CONV:
                    sp.wait_ge(qkv_done, NT * (m + 1))
                else:
                    sp.wait_ge(conv_done, 3 * (m - CONV + 1))
                for c, part in enumerate((1, 2, 0)):
                    col = W * part + P * m
                    src = w_in_d[0, :, col:col + P].rearrange("(k p) c -> p k c", p=P)
                    dst = unit_piece(u, c, lo_raw).rearrange("p (k c) -> p k c", k=KD)
                    sp.dma_start(dst, src).then_inc(unit_loaded[u], 16)
            for g in range(2):
                u = OUT + g
                sp.wait_ge(conv_done, 3 * (u - 3 - CONV + 1))
                src = w_out_d[0, W * g:W * g + W, :].rearrange("(k p) c -> p k c", p=P)
                dst = lo_raw[u % 3].rearrange("p (k c) -> p k c", k=KW)
                sp.dma_start(dst, src).then_inc(unit_loaded[u], 16)
            def load_item(pair, i, ahead=0):
                dst = down_rows(i) if i % EXPERT_SLOTS >= ROUNDS * ROUND_SLOTS else slot_rows(i)
                src = item_source(pair, 2 * ahead + i // EXPERT_SLOTS, i % EXPERT_SLOTS)
                sp.dma_start(dst, src).then_inc(slot_loaded[item_block(i)], 16)

            def refill(pair, i):
                sp.wait_ge(slots_used, pair * PAIR_SLOTS + (FRONT_USES + i + 1))
                ahead, item = item_after(i)
                load_item(pair, item, ahead)

            for i in FIRST_ITEMS:
                b = item_block(i)
                sp.wait_ge(slots_used, 6 if b < 6 else 12 if b < 12 else FRONT_USES)
                load_item(0, i)
            with sp.Fori(0, PAIRS - 1) as pair:
                for i in range(PAIR_SLOTS):
                    refill(pair, i)
            for i in range(PAIR_SLOTS):
                if item_after(i)[0] == 0:
                    refill(PAIRS - 1, i)
            sp.wait_ge(slots_used, (PAIRS - 1) * PAIR_SLOTS + FRONT_USES
                       + (RING_ITEMS[2 * RING] + 1))
            sp.dma_start(g_final, g_final_d.partition_broadcast(P)).then_inc(g_final_loaded, 16)
            for t in range(NT):
                for n, ready in enumerate((final_left_ready, final_right_ready)):
                    sp.wait_ge(ready, t + 1)
                    sp.dma_start(out_d[0, P * t:P * t + P, B * n:B * n + B],
                                 h2[:, t, B * n:B * n + B]).then_inc(out_stored, 16)
            sp.wait_ge(out_stored, 2 * 16 * NT)

        @block.gpsimd
        def _(pool):
            steps = [0]

            def step(ins):
                steps[0] += 1
                ins.then_inc(pool_step, 1)
                pool.wait_ge(pool_step, steps[0])

            pool.memset(eps[:, :], RMS_EPS).then_inc(eps_ready, 1)
            step(pool.memset(ident[:, :], 0.0))
            pool.affine_select(out=ident[:, :], in_=ident[:, :], compare_op=ALU.not_equal, fill=1.0,
                               base=0, pattern=[[-1, P]], channel_multiplier=1).then_inc(consts_ready, 1)
            pool.memset(ones[:, :], 1.0).then_inc(consts_ready, 1)
            freqs = np.float32(ROPE_THETA) ** (-np.arange(ROT_HALF, dtype=np.float32) / np.float32(ROT_HALF))
            for i in range(ROT_HALF):
                pool.memset(inv_freq[:, i:i + 1], float(freqs[i])).then_inc(consts_ready, 1)
            pool.iota(dist.bitcast(I32), pattern=[[-1, 2 * S - P]], base=S - P,
                      channel_multiplier=1).then_inc(consts_ready, 1)
            pool.memset(router_wide[:, KD * E:], 0.0).then_inc(consts_ready, 1)
            pool.iota(slot_ids[:, :], pattern=[[1, CAP]], base=1, channel_multiplier=0,
                      allow_small_or_imprecise_dtypes=True).then_inc(consts_ready, 1)
            pool.wait_ge(eps_ready, 1)
            pool.wait_ge(consts_ready, 13)
            def unit_lo(u, c0, c1):
                for c in range(c0, c1):
                    pool.wait_ge(hi_ready, pieces_before(u) + c + 1)
                    pool.tensor_tensor(unit_piece(u, c, w_lo), unit_piece(u, c, lo_raw),
                                       unit_piece(u, c, w_hi).bitcast(F32), ALU.subtract).then_inc(pool_lo_ready, 1)

            unit_lo(V, 0, 1)
            unit_lo(V, 2, 3)
            unit_lo(Q, 0, 4)
            pool.wait_ge(pool_lo_ready, 2 + 4)
            pool.wait_ge(xn_turned, 2 * NT)
            pool.memset(kT[64:128, 0], 0.0).then_inc(kT_zeroed, 1)
            pool.memset(kT[0:64, 1], 0.0).then_inc(kT_zeroed, 1)
            pool.wait_ge(kT_zeroed, 2)
            for m in range(KW):
                pool.wait_ge(y_conv_ready, m + 1)
                dst = conv_sq if m == 0 else conv_sq1
                step(pool.tensor_tensor(dst, yT_conv[:, m, :], yT_conv[:, m, :], ALU.mult))
                if m:
                    step(pool.tensor_tensor(conv_sq, conv_sq, conv_sq1, ALU.add))
            pool.sem_inc(conv_sq_ready, 1)
            def score_lo(m):
                pool.wait_ge(score_hi_ready, 2 * m - 1)
                pool.tensor_tensor(q_lo[:, m, :], qT[:, m, :], q_hi[:, m - 1, :].bitcast(F32),
                                   ALU.subtract).then_inc(score_lo_ready, 1)
                pool.wait_ge(score_hi_ready, 2 * m)
                pool.tensor_tensor(k_lo[:, :, m, :], kT[:, :, m, :], k_hi[:, :, m - 1, :].bitcast(F32),
                                   ALU.subtract).then_inc(score_lo_ready, 1)

            score_lo(1)
            score_lo(2)
            unit_lo(OUT, 0, 4)
            score_lo(3)
            unit_lo(OUT + 1, 0, 4)
            pool.wait_ge(pool_lo_ready, 2 + 4 + 4 + 4)
            pool.wait_ge(scores_done, 2 * UNITS)
            for m in range(KW):
                pool.wait_ge(y_attn_ready, NT * (m + 1))
                dst = attn_sq if m == 0 else attn_sq1
                step(pool.tensor_tensor(dst, yT_attn[:, m, :], yT_attn[:, m, :], ALU.mult))
                if m:
                    step(pool.tensor_tensor(attn_sq, attn_sq, attn_sq1, ALU.add))
            pool.sem_inc(attn_sq_ready, 1)
            pool.wait_ge(g_final_loaded, 16)
            for n, t in LAST_PUTS:
                pool.wait_ge(x_added, LAST_ADDS + last_add(n, t))
                part = slice(B * n, B * n + B)
                pool.tensor_tensor(h2[:, t, part], x_sb[:, t, part], g_final[:, part], ALU.mult).then_inc(gained, 1)

        @block.scalar
        def _(act):
            act.dma_start(mix_rows, g_mix_d[0].rearrange("(c p) -> c p", p=P)).then_inc(g_mix_loaded, 16)

            waited_tables = [0]

            def sqrt_table():
                act.wait_ge(eps_ready, 1)
                if waited_tables[0]:
                    act.wait_ge(table_ready, waited_tables[0])
                waited_tables[0] += 1
                act.activation(eps_root[:, :], eps[:, :], ACT.Sqrt).then_inc(table_ready, 1)

            def token_root(n):
                act.wait_ge(squared, n + 1)
                act.activation(norm[:, n % 4, 1, 0:1], sums[:, n:n + 1], ACT.Sqrt, bias=eps[:, :],
                               scale=1.0 / D).then_inc(root_ready, 1)

            def channel_root(n):
                act.wait_ge(var_ready, n + 1)
                act.activation(wide_norm[:, n, 1, :], wide_norm[:, n, 0, :], ACT.Sqrt).then_inc(wide_root_ready, 1)

            sqrt_table()

            def square(t):
                act.wait_ge(x_loaded[t], 16)
                act.activation(xn[:, t, :], x_sb[:, t, :], ACT.Square,
                               accum_out=sums[:, t:t + 1]).then_inc(squared, 1)

            def unit_hi(u, c0, c1):
                for c in range(c0, c1):
                    if c == c0:
                        act.wait_ge(unit_loaded[u], 16 * (3 if CONV <= u < OUT else 1))
                    if (u, c) == (V, 2):
                        act.wait_ge(v_rest_loaded, 16)
                    act.activation(unit_piece(u, c, w_hi), unit_piece(u, c, lo_raw), ACT.Copy).then_inc(hi_ready, 1)

            def hT_hi_make(t):
                act.wait_ge(mix_gains_ready, 1)
                for i in range(2):
                    act.wait_ge(xn_turned, 2 * t + i + 1)
                    for k in range(4 * i, 4 * i + 4):
                        ins = act.activation(hT_hi[:, k, P * t:P * t + P], turned_h(t, k), ACT.Copy,
                                             scale=mix_gains[:, k:k + 1])
                    ins.then_inc(hT_hi_ready, 1)

            def v_copy(t):
                act.wait_ge(qkv_done, t + 1)
                act.activation(v_sb[:, t, :], bank[:, t % 3, :], ACT.Copy).then_inc(item_copied, 1)

            def qk_copy(j):
                n = NT + j
                act.wait_ge(qkv_done, n + 1)
                if j == 0:
                    act.wait_ge(xn_ready, NT)
                if j >= STAGES:
                    act.wait_ge(qk_turned, j - STAGES + 1)
                act.activation(stage[j % STAGES], bank[:, n % 3, :], ACT.Copy,
                               scale=HEAD_DIM ** -0.5 if j < NT else 1.0).then_inc(item_copied, 1)

            def qT_copy(t):
                act.wait_ge(qk_turned, t + 1)
                act.activation(qT[:, :, P * t:P * t + P],
                               bank[:, 6 + t % 2, :].rearrange("p (m s) -> p m s", m=KW), ACT.Copy).then_inc(qT_ready, 1)

            def c_copy(m):
                act.wait_ge(conv_done, 3 * m + 1)
                if m >= 2:
                    act.wait_ge(y_conv_ready, m - 1)
                act.activation(c_buf[m % 2], bank[:, conv_bank(m), :], ACT.Copy).then_inc(c_copied, 1)

            square(0)
            token_root(0)
            unit_hi(V, 0, 1)
            hT_hi_make(0)
            square(1)
            token_root(1)
            unit_hi(V, 1, 4)
            hT_hi_make(1)
            square(2)
            token_root(2)
            v_copy(0)
            hT_hi_make(2)
            square(3)
            token_root(3)
            v_copy(1)
            hT_hi_make(3)
            unit_hi(Q, 0, 4)
            v_copy(2)
            act.wait_ge(turns_ready, 1)
            act.activation(sin_cos[:, :], reduced[:, :], ACT.Sin).then_inc(sin_ready, 1)
            v_copy(3)
            qk_copy(0)
            unit_hi(K, 0, 2)
            qk_copy(1)
            qT_copy(0)
            unit_hi(K, 2, 4)
            qk_copy(2)
            qT_copy(1)
            qk_copy(3)
            qT_copy(2)
            unit_hi(CONV, 0, 3)
            qk_copy(4)
            qT_copy(3)
            qk_copy(5)
            qk_copy(6)
            unit_hi(CONV + 1, 0, 3)
            qk_copy(7)
            for m in range(KW):
                if m == 0:
                    act.wait_ge(qk_turned, 2 * NT)
                c_copy(m)
                if m < 2:
                    unit_hi(CONV + m + 2, 0, 3)
                elif m == 2:
                    unit_hi(OUT, 0, 4)

            def score_hi(m):
                if m == SPLIT_FROM:
                    act.wait_ge(conv_done, 3 * KW)
                    act.wait_ge(kT_ready, 2 * NT)
                    act.wait_ge(qT_ready, NT)
                act.activation(q_hi[:, m - 1, :], qT[:, m, :], ACT.Copy).then_inc(score_hi_ready, 1)
                act.activation(k_hi[:, :, m - 1, :], kT[:, :, m, :], ACT.Copy).then_inc(score_hi_ready, 1)

            def reload_x(t):
                act.dma_start(x_sb[:, t, :], x_d[0, P * t:P * t + P, :]).then_inc(x_loaded[t], 16)

            score_hi(1)
            for i in range(UNITS + 2):
                if i in (1, 5):
                    score_hi(2 if i == 1 else 3)
                if i < UNITS:
                    act.wait_ge(neg_ready, i + 1)
                    for h in range(2):
                        s = scores[i % 3][:, h, :]
                        c = 2 * i + h
                        act.activation(s, s, ACT.Exp, bias=neg_max[:, c:c + 1],
                                       accum_out=row_sum[:, c:c + 1]).then_inc(exp_done, 1)
                if i == UNITS:
                    sqrt_table()
                    channel_root(0)
                if i >= 2:
                    u = i - 2
                    act.wait_ge(prob_turned, u + 1)
                    act.activation(probT[u % 2].rearrange("p (b c) -> p b c", b=2), bank[:, 4:6, :],
                                   ACT.Copy).then_inc(probT_ready, 1)
                    if u == UNITS - 4:
                        act.wait_ge(conv_sums_done, 1)
                        reload_x(3)
                    if u >= UNITS - 3:
                        reload_x(u % 3)
                if 2 <= i < 2 + KW:
                    m = i - 2
                    act.activation(yc_hi[:, m, :], yT_conv[:, m, :], ACT.Copy,
                                   scale=columns[:, 12 + m:13 + m]).then_inc(yc_hi_ready, 1)
                if 2 + KW <= i < 6 + KW:
                    unit_hi(OUT + 1, i - 2 - KW, i - 1 - KW)
            act.dma_start(g_ffn, g_ffn_d[0].partition_broadcast(P)).then_inc(g_ffn_loaded, 16)
            for m in range(KW):
                act.wait_ge(y_attn_ready, NT * (m + 1))
                act.activation(ya_hi[:, m, :], yT_attn[:, m, :], ACT.Copy,
                               scale=columns[:, 16 + m:17 + m]).then_inc(ya_hi_ready, 1)
            channel_root(1)

            def x2_half(t):
                act.wait_ge(x2_turned, 2 * t + 1)
                act.activation(x2T[t % 2][:, 0:512], bank[:, 4 + 2 * (t % 2), :], ACT.Copy).then_inc(x2T_ready, 1)

            for t in range(NT):
                if t:
                    x2_half(t - 1)
                act.wait_ge(mix_added, 2 * NT + 2 * t + 2)
                act.activation(h2[:, t, :], x_sb[:, t, :], ACT.Square,
                               accum_out=sums[:, NT + t:NT + t + 1]).then_inc(squared, 1)
                token_root(NT + t)
                if t == NT - 1:
                    x2_half(t)
            act.wait_ge(shifted_ready, 1)
            act.activation(aff[:, :, :], aff[:, :, :], ACT.Exp).then_inc(aff_exp, 1)

            def expert_pair(pair):
                act.wait_ge(gathered, pair * 2 + 1)
                act.activation(xeT[:, 0:4, :], bank[:, 6, :].rearrange("p (k s) -> p k s", k=4),
                               ACT.Copy).then_inc(xeT_low_ready, 1)
                for j in range(2):
                    for r in range(ROUNDS):
                        n = 2 * j + r
                        act.wait_ge(slots_used, pair * PAIR_SLOTS
                                    + (FRONT_USES + EXPERT_SLOTS * j + ROUND_SLOTS * (r + 1)))
                        act.wait_ge(hid_ready, pair * 4 + (n + 1))
                        act.activation(silu[r], bank[:, r, :], ACT.Silu).then_inc(silu_ready, 1)
                    for r in range(ROUNDS):
                        act.wait_ge(hid_turned, pair * 4 + (2 * j + r + 1))
                        dst = hidT[:, 8 * r:8 * r + 8, :].rearrange("p (c b) s -> p b c s", c=2)
                        src = bank[:, 5, :].rearrange("p (b c s) -> p b c s", b=4, c=2)
                        act.activation(dst, src, ACT.Copy).then_inc(hidT_ready, 1)
                    for n in range(2):
                        act.wait_ge(slots_used, pair * PAIR_SLOTS + down_uses(j, n))
                        act.activation(y_pair[CAP * j:CAP * j + CAP, B * n:B * n + 256], bank[0:64, 4 + n, 0:256],
                                       ACT.Copy).then_inc(y_ready, 1)

            with act.Fori(0, PAIRS - 1) as pair:
                expert_pair(pair)
            expert_pair(PAIRS - 1)
            sqrt_table()

            def last_square(t):
                act.wait_ge(x_added, LAST_ADDS + last_add(1, t))
                act.activation(block_of(2 + t // 2)[:, D * (t % 2):D * (t % 2) + D], x_sb[:, t, :], ACT.Square,
                               accum_out=sums[:, 2 * NT + t:2 * NT + t + 1]).then_inc(squared, 1)
                token_root(2 * NT + t)

            def last_scale(t):
                act.wait_ge(inverse_ready, t + 1)
                act.wait_ge(gained, last_gain(0, t))
                act.activation(h2[:, t, 0:B], h2[:, t, 0:B], ACT.Copy,
                               scale=small[:, 0, t:t + 1]).then_inc(final_left_ready, 1)

            last_square(0)
            last_square(1)
            last_scale(0)
            last_square(2)
            last_scale(1)
            last_square(3)
            last_scale(2)
            last_scale(3)

        @block.vector
        def _(dve):
            steps = [0]

            def step(ins):
                steps[0] += 1
                ins.then_inc(dve_step, 1)
                dve.wait_ge(dve_step, steps[0])

            def inverse_root(n, out=None):
                var, rt, inv, tmp = (norm[:, n % 4, i, :] for i in range(4))
                dve.wait_ge(squared, n + 1)
                step(dve.tensor_scalar(var, sums[:, n:n + 1], 1.0 / D, RMS_EPS, ALU.mult, ALU.add))
                dve.wait_ge(root_ready, n + 1)
                step(dve.reciprocal(inv, rt))
                step(dve.scalar_tensor_tensor(out=tmp, in0=inv, scalar=var, in1=inv, op0=ALU.mult, op1=ALU.mult))
                step(dve.tensor_scalar(tmp, tmp, -0.5, 1.5, ALU.mult, ALU.add))
                if out is None:
                    return inv, tmp
                step(dve.tensor_tensor(out, inv, tmp, ALU.mult))
                return out

            def channel_inverse(n, totals):
                var, rt, inv, tmp = (wide_norm[:, n, i, :] for i in range(4))
                dve.tensor_scalar(var, totals, 1.0 / W, RMS_EPS, ALU.mult, ALU.add).then_inc(var_ready, 1)
                dve.wait_ge(wide_root_ready, n + 1)
                step(dve.reciprocal(inv, rt))
                step(dve.tensor_tensor(tmp, inv, inv, ALU.mult))
                step(dve.tensor_tensor(tmp, tmp, var, ALU.mult))
                step(dve.tensor_scalar(tmp, tmp, -0.5, 1.5, ALU.mult, ALU.add))
                step(dve.tensor_tensor(inv, inv, tmp, ALU.mult))
                return inv

            def first_norm(t):
                inv, more = inverse_root(t)
                dve.tensor_scalar(xn[:, t, :], x_sb[:, t, :], inv, more, ALU.mult, ALU.mult).then_inc(xn_ready, 1)

            def hT_lo_make(t):
                for i in range(2):
                    dve.wait_ge(hT_hi_ready, 2 * t + i + 1)
                    for k in range(4 * i, 4 * i + 4):
                        ins = dve.scalar_tensor_tensor(out=hT_lo[:, k, P * t:P * t + P], in0=turned_h(t, k),
                                                       scalar=mix_gains[:, k:k + 1],
                                                       in1=hT_hi[:, k, P * t:P * t + P].bitcast(F32),
                                                       op0=ALU.mult, op1=ALU.subtract)
                    ins.then_inc(hT_lo_ready, 1)

            def unit_lo(u, c0, c1):
                for c in range(c0, c1):
                    dve.wait_ge(hi_ready, pieces_before(u) + c + 1)
                    dve.tensor_tensor(unit_piece(u, c, w_lo), unit_piece(u, c, lo_raw),
                                      unit_piece(u, c, w_hi).bitcast(F32), ALU.subtract).then_inc(lo_ready, 1)

            first_norm(0)
            dve.wait_ge(mix_gains_turned, 1)
            dve.tensor_copy(mix_gains[:, :], bank[:, 3, 0:KD]).then_inc(mix_gains_ready, 1)
            dve.wait_ge(mix_gains_ready, 1)
            hT_lo_make(0)
            first_norm(1)
            unit_lo(V, 1, 2)
            unit_lo(V, 3, 4)
            hT_lo_make(1)
            first_norm(2)
            hT_lo_make(2)
            first_norm(3)
            hT_lo_make(3)
            dve.wait_ge(rows_loaded, 80)
            dve.tensor_copy(pos_rows, pos_int.bitcast(I32)).then_inc(pos_ready, 1)
            dve.wait_ge(rows_turned, 2)
            dve.tensor_copy(columns[:, :], bank[:, 3, 8:40]).then_inc(columns_ready, 1)

            dve.wait_ge(consts_ready, 13)
            dve.wait_ge(columns_ready, 1)
            ang = angles[:, :].rearrange("p (t i) -> p t i", t=NT)
            step(dve.tensor_tensor(ang, columns[:, 28:32].unsqueeze(2).to_broadcast([P, NT, ROT_HALF]),
                                   inv_freq[:, :].unsqueeze(1).to_broadcast([P, NT, ROT_HALF]), ALU.mult))
            half = NT * ROT_HALF
            for i in range(2):
                step(dve.tensor_scalar(turns[:, half * i:half * i + half], angles[:, :],
                                       1.0 / (2.0 * math.pi), 0.25 * i, ALU.mult, ALU.add))
            step(dve.tensor_scalar(turns[:, :], turns[:, :], ROUND, None, ALU.add))
            step(dve.tensor_scalar(turns[:, :], turns[:, :], ROUND, None, ALU.subtract))
            for i in range(2):
                dst = reduced[:, half * i:half * i + half]
                src = angles[:, :]
                for part in TURN_PARTS:
                    step(dve.scalar_tensor_tensor(out=dst, in0=turns[:, half * i:half * i + half], scalar=-part,
                                                  in1=src, op0=ALU.mult, op1=ALU.add))
                    src = dst
            step(dve.tensor_scalar(reduced[:, half:2 * half], reduced[:, half:2 * half], math.pi / 2, None, ALU.add))
            dve.tensor_scalar(reduced[:, :], reduced[:, :], PI_INSIDE, -PI_INSIDE,
                              ALU.min, ALU.max).then_inc(turns_ready, 1)

            dist_i, a_i = dist.bitcast(I32), mask_a.bitcast(I32)
            reach = [float((window // 2 // dil * dil) ** 2) for window, dil in PATTERNS]

            def strip_start():
                step(dve.tensor_tensor(mask_b, dist_i, dist_i, ALU.mult))
                step(dve.tensor_scalar(strip[:, :], mask_b, reach[0], None, ALU.is_le))

            def strip_add(i):
                for (window, dil), far in [(PATTERNS[i], reach[i])]:
                    step(dve.tensor_scalar(a_i, dist_i, dil - 1, None, ALU.bitwise_and))
                    step(dve.tensor_scalar(mask_a, a_i, 0.0, None, ALU.is_equal))
                    step(dve.scalar_tensor_tensor(out=mask_a, in0=mask_b, scalar=far, in1=mask_a,
                                                  op0=ALU.is_le, op1=ALU.mult))
                    step(dve.tensor_tensor(strip[:, :], strip[:, :], mask_a, ALU.add))

            def strip_end():
                step(dve.tensor_scalar(mask_a, strip[:, :], 2.0, math.log(2.0), ALU.is_equal, ALU.mult))
                step(dve.tensor_scalar(mask_b, strip[:, :], 3.0, math.log(3.0), ALU.is_equal, ALU.mult))
                step(dve.tensor_tensor(mask_a, mask_a, mask_b, ALU.add))
                step(dve.tensor_scalar(strip[:, :], strip[:, :], 0.0, MASKED, ALU.is_equal, ALU.mult))
                dve.tensor_tensor(strip[:, :], strip[:, :], mask_a, ALU.add).then_inc(strip_ready, 1)

            def rope(j):
                t = j % NT
                heads = stage[j % STAGES].rearrange("p (h c) -> p h c", c=HEAD_DIM)
                first, second = heads[:, :, 0:ROT_HALF], heads[:, :, ROT_HALF:2 * ROT_HALF]
                sin, cos = (sin_cos[:, half * i + ROT_HALF * t:half * i + ROT_HALF * t + ROT_HALF]
                            .unsqueeze(1).to_broadcast([P, NH, ROT_HALF]) for i in range(2))
                dve.wait_ge(item_copied, NT + j + 1)
                if j:
                    dve.wait_ge(rope_done, 2 * j)
                step(dve.tensor_tensor(rot[:, 0], first, cos, ALU.mult))
                step(dve.tensor_tensor(rot[:, 1], second, sin, ALU.mult))
                step(dve.tensor_tensor(rot[:, 2], second, cos, ALU.mult))
                step(dve.tensor_tensor(rot[:, 3], first, sin, ALU.mult))
                dve.tensor_tensor(first, rot[:, 0], rot[:, 1], ALU.subtract).then_inc(rope_done, 1)
                dve.tensor_tensor(second, rot[:, 2], rot[:, 3], ALU.add).then_inc(rope_done, 1)

            def kT_copy(t):
                dve.wait_ge(qk_turned, NT + t + 1)
                if t == 0:
                    dve.wait_ge(kT_zeroed, 2)
                for h in range(2):
                    half_rows = slice(HEAD_DIM * h, HEAD_DIM * h + HEAD_DIM)
                    dve.tensor_copy(kT[half_rows, h, :, P * t:P * t + P],
                                    bank[half_rows, 6 + t % 2, :].rearrange("p (m s) -> p m s", m=KW)).then_inc(kT_ready, 1)

            def conv(m):
                base = conv_bank(m)
                z = z_buf[m % 2]
                y = yT_conv[:, m, :]
                tap = [columns[:, KW * i + m:KW * i + m + 1] for i in range(TAPS)]
                dve.wait_ge(c_copied, m + 1)
                if m < 2:
                    step(dve.memset(z[:, 0:1], 0.0))
                    step(dve.memset(z[:, S + 1:S + 2], 0.0))
                dve.wait_ge(conv_done, 3 * m + 2)
                step(dve.tensor_tensor(z[:, 1:S + 1], c_buf[m % 2], bank[:, base + 1, :], ALU.mult))
                step(dve.tensor_scalar(y, z[:, 0:S], tap[0], None, ALU.mult))
                step(dve.scalar_tensor_tensor(out=y, in0=z[:, 1:S + 1], scalar=tap[1], in1=y,
                                              op0=ALU.mult, op1=ALU.add))
                step(dve.scalar_tensor_tensor(out=y, in0=z[:, 2:S + 2], scalar=tap[2], in1=y,
                                              op0=ALU.mult, op1=ALU.add))
                dve.wait_ge(conv_done, 3 * m + 3)
                dve.tensor_tensor(y, y, bank[:, base + 2, :], ALU.mult).then_inc(y_conv_ready, 1)

            dve.wait_ge(sin_ready, 1)
            rope(0)
            unit_lo(K, 0, 2)
            rope(1)
            unit_lo(K, 2, 4)
            strip_start()
            rope(2)
            strip_add(1)
            rope(3)
            unit_lo(CONV, 0, 3)
            rope(4)
            strip_add(2)
            rope(5)
            kT_copy(0)
            strip_end()
            rope(6)
            kT_copy(1)
            unit_lo(CONV + 1, 0, 3)
            rope(7)
            dve.wait_ge(rope_done, 4 * NT)
            kT_copy(2)
            kT_copy(3)
            for m in range(KW):
                conv(m)
                if m < 2:
                    unit_lo(CONV + m + 2, 0, 3)
            dve.wait_ge(router_loaded, 16)
            dve.tensor_tensor(router[:, :].rearrange("p (k e) -> p k e", k=KD),
                              router[:, :].rearrange("p (k e) -> p k e", k=KD),
                              columns[:, 20:28].unsqueeze(2).to_broadcast([P, KD, E]),
                              ALU.mult).then_inc(router_scaled, 1)

            def take_y(u):
                m, t = divmod(u, NT)
                dve.wait_ge(pv_done, u + 1)
                dve.tensor_copy(yT_attn[:, m, P * t:P * t + P], bank[:, 6 + u % 2, 0:P]).then_inc(y_attn_ready, 1)

            for i in range(UNITS + 1):
                if i < UNITS:
                    t = i % NT
                    seen = strip[:, S - P - P * t:2 * S - P - P * t]
                    for h in range(2):
                        c = 2 * i + h
                        dve.wait_ge(scores_done, c + 1)
                        dve.tensor_tensor_reduce(out=scores[i % 3][:, h, :], in0=bank[:, score_bank(i) + h, :],
                                                 in1=seen, scale=1.0, scalar=-3e38, op0=ALU.add, op1=ALU.max,
                                                 accum_out=row_max[:, c:c + 1]).then_inc(max_ready, 1)
                    dve.wait_ge(max_ready, 2 * i + 2)
                    dve.tensor_scalar(neg_max[:, 2 * i:2 * i + 2], row_max[:, 2 * i:2 * i + 2], -1.0, None,
                                      ALU.mult).then_inc(neg_ready, 1)
                if i >= 1:
                    u = i - 1
                    dve.wait_ge(exp_done, 2 * u + 2)
                    dve.reciprocal(row_inv[:, 2 * u:2 * u + 2], row_sum[:, 2 * u:2 * u + 2]).then_inc(inv_ready, 1)
                    dve.wait_ge(inv_ready, u + 1)
                    for h in range(2):
                        s = scores[u % 3][:, h, :]
                        dve.tensor_scalar(s, s, row_inv[:, 2 * u + h:2 * u + h + 1], None,
                                          ALU.mult).then_inc(prob_ready, 1)
                if i >= 3:
                    take_y(i - 3)
                if 3 <= i < 3 + KW:
                    m = i - 3
                    dve.wait_ge(yc_hi_ready, m + 1)
                    dve.scalar_tensor_tensor(out=yc_lo[:, m, :], in0=yT_conv[:, m, :],
                                             scalar=columns[:, 12 + m:13 + m], in1=yc_hi[:, m, :].bitcast(F32),
                                             op0=ALU.mult, op1=ALU.subtract).then_inc(yc_lo_ready, 1)

            def add_mix(o, inv):
                g, t, n = mix_place(o)
                xs = x_sb[:, t, B * n:B * n + B]
                dve.wait_ge(mix_done, o + 1)
                if g:
                    dve.wait_ge(mix_added, 2 * NT)
                else:
                    dve.wait_ge(x_loaded[t], 32)
                dve.scalar_tensor_tensor(out=xs, in0=bank[:, o % 3, :], scalar=inv[:, t:t + 1], in1=xs,
                                         op0=ALU.mult, op1=ALU.add).then_inc(mix_added, 1)

            inv_conv = channel_inverse(0, bank[:, 7, P:P + 96 * NT:96])
            add_mix(0, inv_conv)
            take_y(UNITS - 2)
            add_mix(1, inv_conv)
            take_y(UNITS - 1)
            for m in range(KW):
                dve.wait_ge(ya_hi_ready, m + 1)
                dve.scalar_tensor_tensor(out=ya_lo[:, m, :], in0=yT_attn[:, m, :],
                                         scalar=columns[:, 16 + m:17 + m], in1=ya_hi[:, m, :].bitcast(F32),
                                         op0=ALU.mult, op1=ALU.subtract).then_inc(ya_lo_ready, 1)
                add_mix(2 + m, inv_conv)
            for o in range(2 + KW, 2 * NT):
                add_mix(o, inv_conv)
            dve.wait_ge(attn_sums_done, NT)
            inv_attn = channel_inverse(1, bank[:, 3, 0:96 * NT:96])
            dve.wait_ge(g_ffn_loaded, 16)

            def x2_half(t):
                dve.wait_ge(x2_turned, 2 * t + 2)
                dve.tensor_copy(x2T[t % 2][:, 512:1024], bank[:, 5 + 2 * (t % 2), :]).then_inc(x2T_ready, 1)

            for t in range(NT):
                add_mix(2 * NT + 2 * t, inv_attn)
                if t:
                    x2_half(t - 1)
                add_mix(2 * NT + 2 * t + 1, inv_attn)
                if t == NT - 1:
                    x2_half(t)
                inv = inverse_root(NT + t, out=small[:, 3, t:t + 1])
                dve.scalar_tensor_tensor(out=h2[:, t, :], in0=x_sb[:, t, :], scalar=inv, in1=g_ffn,
                                         op0=ALU.mult, op1=ALU.mult).then_inc(h2_ready, 1)

            products = bank[:, 3, 0:96 * NT].rearrange("p (t c) -> p t c", t=NT)[:, :, 0:E]
            dve.wait_ge(logits_done, NT)
            step(dve.tensor_tensor(aff[:, :, :], products, small[:, 3, :].unsqueeze(2).to_broadcast([P, NT, E]),
                                   ALU.mult))
            step(dve.tensor_reduce(small[:, 0, :], aff[:, :, :], AX.X, ALU.max))
            dve.tensor_tensor(aff[:, :, :], aff[:, :, :], small[:, 0, :].unsqueeze(2).to_broadcast([P, NT, E]),
                              ALU.subtract).then_inc(shifted_ready, 1)
            dve.wait_ge(aff_exp, 1)
            step(dve.tensor_reduce(small[:, 1, :], aff[:, :, :], AX.X, ALU.add))
            step(dve.reciprocal(small[:, 2, :], small[:, 1, :]))
            dve.tensor_tensor(aff[:, :, :], aff[:, :, :], small[:, 2, :].unsqueeze(2).to_broadcast([P, NT, E]),
                              ALU.mult).then_inc(aff_ready, 1)

            dve.memset(top_ones, 1.0).then_inc(top_ones_ready, 1)
            dve.wait_ge(top_ones_ready, 1)

            dve.wait_ge(aff_turned, NT)
            for i in range(CAP // 8):
                left = top_row[i % 2] if i else bank[0:E, 4, :]
                dve.max(top8[:, :], left).then_inc(top8_ready, 1)
                dve.wait_ge(top8_ready, i + 1)
                step(dve.match_replace(out=top_row[(i + 1) % 2], in_to_replace=top8[:, :],
                                       in_values=left, imm_value=-1.0))
            taken, other, chosen = top_row[(CAP // 8) % 2], top_row[(CAP // 8 + 1) % 2], top_row[2]
            step(dve.tensor_scalar(chosen, taken, -1.0, None, ALU.is_equal))
            step(dve.tensor_tensor_scan(taken, top_ones, chosen, 0.0, ALU.mult, ALU.add))
            dve.tensor_tensor(other, taken, chosen, ALU.mult).then_inc(slot_row_ready, 1)
            dve.wait_ge(slot_row_turned, NT)
            step(dve.tensor_copy(slot_of[:, :, :], bank[:, 5, 0:NT * E].rearrange("p (t e) -> p t e", t=NT)))
            dve.sem_inc(hid_ready, 2)

            def expert_pair(pair):
                places = slot_of[:, :, bass.ds(pair * 2, 2)]
                gates = aff[:, :, bass.ds(pair * 2, 2)]
                dve.tensor_tensor(picks, slot_ids[:, :].unsqueeze(1).unsqueeze(1).to_broadcast([P, NT, 2, CAP]),
                                  places.unsqueeze(3).to_broadcast([P, NT, 2, CAP]),
                                  ALU.is_equal).then_inc(picks_ready, 1)
                dve.wait_ge(picks_ready, pair + 1)
                dve.tensor_tensor(gated, picks, gates.unsqueeze(3).to_broadcast([P, NT, 2, CAP]),
                                  ALU.mult).then_inc(gated_ready, 1)
                dve.wait_ge(gathered, pair * 2 + 2)
                dve.tensor_copy(xeT[:, 4:8, :],
                                bank[:, 7, :].rearrange("p (k s) -> p k s", k=4)).then_inc(xeT_high_ready, 1)
                dve.wait_ge(gated_turned, pair + 1)
                dve.tensor_copy(putT, bank[:, 5, :]).then_inc(putT_ready, 1)
                for j in range(2):
                    for r in range(ROUNDS):
                        dve.wait_ge(silu_ready, pair * 4 + (2 * j + r + 1))
                        dve.tensor_tensor(hid[r], silu[r], bank[:, 2 + r, :], ALU.mult).then_inc(hid_ready, 1)
                    for n in range(2):
                        dve.wait_ge(slots_used, pair * PAIR_SLOTS + down_uses(j, n))
                        dve.tensor_copy(y_pair[CAP * j:CAP * j + CAP, B * n + 256:B * n + B],
                                        bank[64:128, 4 + n, 0:256]).then_inc(y_ready, 1)
                        if not isinstance(pair, int) or (j, n) != (1, 0):
                            continue
                        for i in range(3):
                            last_sum(i)

            def last_sum(i):
                n, t = LAST_PUTS[i]
                xs = x_sb[:, t, B * n:B * n + B]
                dve.wait_ge(put_done, LAST_ADDS + i + 1)
                dve.tensor_tensor(xs, xs, bank[:, last_bank(n, t), :], ALU.add).then_inc(x_added, 1)

            with dve.Fori(0, PAIRS - 1) as pair:
                expert_pair(pair)
                for o in range(2 * NT):
                    t, n = divmod(o, 2)
                    xs = x_sb[:, t, B * n:B * n + B]
                    dve.wait_ge(put_done, pair * (2 * NT) + (o + 1))
                    dve.tensor_tensor(xs, xs, bank[:, 6 + n, :], ALU.add).then_inc(x_added, 1)
            expert_pair(PAIRS - 1)

            def last_norm(t):
                inv = small[:, 0, t:t + 1]
                inverse_root(2 * NT + t, out=inv)
                dve.sem_inc(inverse_ready, 1)
                dve.wait_ge(gained, last_gain(1, t))
                dve.tensor_scalar(h2[:, t, B:D], h2[:, t, B:D], inv, None, ALU.mult).then_inc(final_right_ready, 1)

            last_sum(3)
            last_sum(4)
            last_norm(0)
            last_sum(5)
            last_norm(1)
            last_sum(6)
            last_sum(7)
            last_norm(2)
            last_norm(3)

        @block.tensor
        def _(pe):
            def keep_warm(n, count):
                for _ in range(count):
                    pe.transpose(bank[:, n, 0:P], ident[:, :], ident[:, :])

            pe.wait_ge(consts_ready, 2)
            keep_warm(2, 14)
            pe.wait_ge(g_mix_loaded, 16)
            pe.transpose(bank[:, 3, 0:KD], mix_rows, ident[0:KD, 0:KD]).then_inc(mix_gains_turned, 1)

            def h_turn(t):
                pe.wait_ge(xn_ready, t + 1)
                if t >= 2:
                    pe.wait_ge(hT_lo_ready, 2 * t - 2)
                for k in range(KD):
                    mm = pe.transpose(turned_h(t, k), xn[:, t, P * k:P * k + P], ident[:, :])
                    if k % 4 == 3:
                        mm.then_inc(xn_turned, 1)

            def rows_turn():
                pe.wait_ge(mix_gains_ready, 1)
                pe.wait_ge(rows_loaded, 80)
                pe.transpose(bank[:, 3, 8:36], gain_rows, ident[0:28, 0:28]).then_inc(rows_turned, 1)
                pe.wait_ge(pos_ready, 1)
                pe.transpose(bank[:, 3, 36:40], pos_rows, ident[0:NT, 0:NT]).then_inc(rows_turned, 1)

            def qkv(n):
                u, t = divmod(n, NT)
                if u == 0:
                    pe.wait_ge(hT_lo_ready, 2 * t + 2)
                if n >= 3:
                    pe.wait_ge(item_copied, n - 2)
                for k in range(KD):
                    if n == 0 and k == 2:
                        h_turn(1)
                    if t == 0 and k % 2 == 0:
                        pe.wait_ge(*lo_wait(u, k // 2))
                    h_hi, h_lo = (part[:, k, P * t:P * t + P] for part in (hT_hi, hT_lo))
                    out = bank[:, n % 3, :]
                    pe.matmul(out, h_hi, unit_k(u, k, w_hi), start=(k == 0), stop=False)
                    pe.matmul(out, h_hi, unit_k(u, k, w_lo), start=False, stop=False)
                    mm = pe.matmul(out, h_lo, unit_k(u, k, w_hi), start=False, stop=(k == KD - 1))
                mm.then_inc(qkv_done, 1)

            def qk_turn(j):
                pe.wait_ge(rope_done, 2 * j + 2)
                if j >= 2:
                    if j - 2 < NT:
                        pe.wait_ge(qT_ready, j - 1)
                    else:
                        pe.wait_ge(kT_ready, 2 * (j - 1 - NT))
                for m in range(KW):
                    mm = pe.transpose(bank[:, 6 + j % 2, P * m:P * m + P],
                                      stage[j % STAGES][:, P * m:P * m + P], ident[:, :])
                mm.then_inc(qk_turned, 1)

            def conv_in(m, i):
                u = CONV + m
                pe.wait_ge(*lo_wait(u, i))
                if i == 0:
                    if m == 0:
                        pe.wait_ge(columns_ready, 1)
                    elif m == 1:
                        pe.wait_ge(item_copied, 3 * NT)
                    else:
                        pe.wait_ge(y_conv_ready, m - 1)
                hi, lo = (unit_piece(u, i, place).rearrange("p (k c) -> p k c", k=KD) for place in (w_hi, w_lo))
                out = bank[:, conv_bank(m) + i, :]
                for k in range(KD):
                    pe.matmul(out, hi[:, k, :], hT_hi[:, k, :], start=(k == 0), stop=False)
                    pe.matmul(out, hi[:, k, :], hT_lo[:, k, :], start=False, stop=False)
                    mm = pe.matmul(out, lo[:, k, :], hT_hi[:, k, :], start=False, stop=(k == KD - 1))
                mm.then_inc(conv_done, 1)

            h_turn(0)
            keep_warm(2, 16)
            qkv(0)
            h_turn(2)
            qkv(1)
            h_turn(3)
            qkv(2)
            rows_turn()
            qkv(3)
            qkv(4)
            for j in range(7):
                qkv(5 + j)
                qk_turn(j)
            conv_in(0, 0)
            qk_turn(7)
            for n in range(1, 3 * KW):
                conv_in(n // 3, n % 3)

            def unit_scores(u):
                m, t = divmod(u, NT)
                if u >= 3:
                    pe.wait_ge(max_ready, 2 * u - 2)
                if m >= SPLIT_FROM and t == 0:
                    pe.wait_ge(score_lo_ready, 2 * m)
                tokens = slice(P * t, P * t + P)
                for h in range(2):
                    out = bank[:, score_bank(u) + h, :]
                    if m < SPLIT_FROM:
                        mm = pe.matmul(out, qT[:, m, tokens], kT[:, h, m, :], start=True, stop=True)
                    else:
                        pe.matmul(out, q_hi[:, m - 1, tokens], k_hi[:, h, m - 1, :], start=True, stop=False)
                        pe.matmul(out, q_hi[:, m - 1, tokens], k_lo[:, h, m, :], start=False, stop=False)
                        mm = pe.matmul(out, q_lo[:, m, tokens], k_hi[:, h, m - 1, :], start=False, stop=True)
                    mm.then_inc(scores_done, 1)

            def mix_group(o):
                g, t, n = mix_place(o)
                if o >= 3:
                    pe.wait_ge(mix_added, o - 2)
                u = OUT + g
                y_hi, y_lo = ((yc_hi, yc_lo), (ya_hi, ya_lo))[g]
                for m in range(KW):
                    if o in (0, 2 * NT):
                        pe.wait_ge(*lo_wait(u, m))
                        pe.wait_ge((yc_lo_ready, ya_lo_ready)[g], m + 1)
                    hi, lo = (unit_piece(u, m, place)[:, B * n:B * n + B] for place in (w_hi, w_lo))
                    tokens = slice(P * t, P * t + P)
                    out = bank[:, o % 3, :]
                    mm = pe.matmul(out, y_hi[:, m, tokens], hi, start=(m == 0), stop=False)
                    if o == 2 * NT and m == 0:
                        mm.then_inc(slots_used, 6)
                    pe.matmul(out, y_hi[:, m, tokens], lo, start=False, stop=False)
                    mm = pe.matmul(out, y_lo[:, m, tokens], hi, start=False, stop=(m == KW - 1))
                mm.then_inc(mix_done, 1)

            def x2_turn(t, chunks=range(KD)):
                for k in chunks:
                    if k % 4 == 0:
                        pe.wait_ge(mix_added, 2 * NT + 2 * t + 1 + k // 4)
                    mm = pe.transpose(bank[:, 4 + 2 * (t % 2) + k // 4, P * (k % 4):P * (k % 4) + P],
                                      x_sb[:, t, P * k:P * k + P], ident[:, :])
                    if t == NT - 1 and k == 0:
                        mm.then_inc(slots_used, 4)
                    if k % 4 == 3:
                        mm.then_inc(x2_turned, 1)

            def route(t):
                pe.wait_ge(x2T_ready, 2 * t + 2)
                if t == 0:
                    pe.wait_ge(var_ready, 2)
                for k in range(KD):
                    mm = pe.matmul(bank[:, 3, 96 * t:96 * t + 96], x2T[t % 2][:, P * k:P * k + P],
                                   router_wide[:, E * k:E * k + 96], start=(k == 0), stop=(k == KD - 1))
                mm.then_inc(logits_done, 1)

            pe.wait_ge(qT_ready, NT)
            pe.wait_ge(kT_ready, 2 * NT)
            for u in range(3):
                unit_scores(u)
                if u == 0:
                    pe.wait_ge(strip_ready, 1)
                    pe.wait_ge(y_conv_ready, KW)
            for u in range(UNITS):
                m = u // NT
                pe.wait_ge(prob_ready, 2 * u + 2)
                if u:
                    pe.wait_ge(probT_ready, u)
                for h in range(2):
                    for k in range(NT):
                        mm = pe.transpose(bank[:, 4 + h, P * k:P * k + P],
                                          scores[u % 3][:, h, P * k:P * k + P], ident[:, :])
                        if (u, h, k) == (UNITS - 3, 0, 0):
                            mm.then_inc(slots_used, 6)
                mm.then_inc(prob_turned, 1)
                if u + 3 < UNITS:
                    unit_scores(u + 3)
                else:
                    o = u + 3 - UNITS
                    pe.wait_ge(max_ready, 2 * UNITS if o == 2 else 2 * UNITS - 2)
                    mix_group(o)
                pe.wait_ge(probT_ready, u + 1)
                if u >= 2:
                    pe.wait_ge(y_attn_ready, u - 1)
                if u == 3:
                    pe.wait_ge(conv_sq_ready, 1)
                    for s in range(NT):
                        mm = pe.matmul(bank[:, 7, P + 96 * s:P + 96 * s + 96], conv_sq[:, P * s:P * s + P],
                                       ones[:, :].to_broadcast([P, 96]), start=True, stop=True)
                    mm.then_inc(conv_sums_done, 1)
                for k in range(NT):
                    for h in range(2):
                        head = 2 * m + h
                        mm = pe.matmul(bank[HEAD_DIM * h:HEAD_DIM * h + HEAD_DIM, 6 + u % 2, 0:P],
                                       v_sb[:, k, HEAD_DIM * head:HEAD_DIM * head + HEAD_DIM],
                                       probT[u % 2][:, 512 * h + P * k:512 * h + P * k + P],
                                       start=(k == 0), stop=(k == NT - 1))
                mm.then_inc(pv_done, 1)

            for o in range(3, 2 * NT):
                if o == 5:
                    pe.wait_ge(attn_sq_ready, 1)
                    for s in range(NT):
                        mm = pe.matmul(bank[:, 3, 96 * s:96 * s + 96], attn_sq[:, P * s:P * s + P],
                                       ones[:, :].to_broadcast([P, 96]), start=True, stop=True)
                        mm.then_inc(attn_sums_done, 1)
                mix_group(o)
            pe.wait_ge(router_scaled, 1)
            for t in range(NT):
                mix_group(2 * NT + 2 * t)
                if t:
                    x2_turn(t - 1)
                mix_group(2 * NT + 2 * t + 1)
                if t == NT - 1:
                    x2_turn(t, range(KD // 2))
                if t:
                    route(t - 1)
            x2_turn(NT - 1, range(KD // 2, KD))
            route(NT - 1)

            pe.wait_ge(aff_ready, 1)
            for t in range(NT):
                pe.transpose(bank[0:E, 4, P * t:P * t + P], aff[:, t, :], ident[:, :]).then_inc(aff_turned, 1)
            for i in range(CAP // 8):
                pe.wait_ge(top8_ready, i + 1)
                keep_warm(6, 12 if i < CAP // 8 - 1 else 24)
            pe.wait_ge(slot_row_ready, 1)
            place_row = top_row[(CAP // 8 + 1) % 2]
            for t in range(NT):
                pe.transpose(bank[:, 5, E * t:E * t + E], place_row[:, P * t:P * t + P],
                             ident[0:E, 0:E]).then_inc(slot_row_turned, 1)
            keep_warm(6, 12)

            def expert_pair(pair, last):
                pe.wait_ge(picks_ready, pair + 1)
                def gather(chunks):
                    for k in chunks:
                        for t in range(NT):
                            mm = pe.matmul(bank[:, 6 + k // 4, P * (k % 4):P * (k % 4) + P],
                                           h2[:, t, P * k:P * k + P], picks[:, t, :, :].rearrange("p j s -> p (j s)"),
                                           start=(t == 0), stop=(t == NT - 1))
                        if k % 4 == 3:
                            mm.then_inc(gathered, 1)

                gather(range(0, 5))
                pe.wait_ge(xeT_low_ready, pair + 1)
                for j in range(2):
                    tokens = slice(CAP * j, CAP * j + CAP)
                    for r in range(ROUNDS):
                        pe.wait_ge(hid_ready, pair * 4 + (2 * j + r + 1))
                        for q in range(ROUND_SLOTS):
                            i = EXPERT_SLOTS * j + ROUND_SLOTS * r + q
                            if i == KD // 2 - 1:
                                gather(range(5, KD))
                            if i == KD // 2:
                                pe.wait_ge(xeT_high_ready, pair + 1)
                            pe.wait_ge(slot_loaded[item_block(i)], item_loads(pair, i))
                            for kk in range(2):
                                k = 2 * (q // 2) + kk
                                for c in range(2):
                                    mm = pe.matmul(bank[64 * c:64 * c + 64, 2 * (q % 2) + r, :], xeT[:, k, tokens],
                                                   slot_rows(i)[:, kk, B * c:B * c + B],
                                                   start=(k == 0), stop=(k == KD - 1))
                            mm.then_inc(slots_used, 1)
                    if j == 0:
                        pe.wait_ge(gated_ready, pair + 1)
                        for t in range(NT):
                            mm = pe.transpose(bank[:, 5, P * t:P * t + P],
                                              gated[:, t, :, :].rearrange("p j s -> p (j s)"), ident[:, :])
                        mm.then_inc(gated_turned, 1)
                    if j:
                        pe.wait_ge(y_ready, pair * 8 + 4)
                    for r in range(ROUNDS):
                        pe.wait_ge(hid_ready, pair * 4 + (2 * j + r + 3))
                        if r == 0 and j == 0:
                            pe.wait_ge(putT_ready, pair + 1)
                        else:
                            pe.wait_ge(hidT_ready, pair * 4 + (2 * j + r))
                        for b in range(4):
                            mm = pe.transpose(bank[:, 5, P * b:P * b + P], hid[r][:, P * b:P * b + P], ident[:, :])
                        mm.then_inc(hid_turned, 1)
                    pe.wait_ge(hidT_ready, pair * 4 + (2 * j + 2))
                    for q in range(F // 256):
                        n, part = divmod(q, F // 512)
                        if last and j and q > F // 512:
                            last_put(q - F // 512 - 1)
                        i = EXPERT_SLOTS * j + ROUNDS * ROUND_SLOTS + q
                        pe.wait_ge(slot_loaded[item_block(i)], item_loads(pair, i))
                        for kk in range(4):
                            f = 4 * part + kk
                            for c in range(2):
                                mm = pe.matmul(bank[64 * c:64 * c + 64, 4 + n, 0:256], hidT[:, f, :],
                                               down_rows(i)[:, kk, 256 * c:256 * c + 256],
                                               start=(f == 0), stop=(f == F // P - 1))
                        mm.then_inc(slots_used, 1)

            def last_put(i):
                n, t = LAST_PUTS[i]
                if i == 0:
                    pe.wait_ge(y_ready, LAST_Y + 6)
                if i == 2:
                    pe.wait_ge(x_added, LAST_ADDS + last_add(0, 0))
                if i == 3:
                    pe.wait_ge(y_ready, LAST_Y + 8)
                if i == 6:
                    pe.wait_ge(x_added, LAST_ADDS + last_add(0, 1))
                pe.matmul(bank[:, last_bank(n, t), :], putT[:, P * t:P * t + P], y_pair[:, B * n:B * n + B],
                          start=True, stop=True).then_inc(put_done, 1)

            LAST_Y = 8 * (PAIRS - 1)
            pe.wait_ge(h2_ready, NT)
            with pe.Fori(0, PAIRS - 1) as pair:
                expert_pair(pair, False)
                pe.wait_ge(y_ready, pair * 8 + 8)
                for o in range(2 * NT):
                    t, n = divmod(o, 2)
                    if o >= 2:
                        pe.wait_ge(x_added, pair * (2 * NT) + (o - 1))
                    pe.matmul(bank[:, 6 + n, :], putT[:, P * t:P * t + P], y_pair[:, B * n:B * n + B],
                              start=True, stop=True).then_inc(put_done, 1)
                pe.wait_ge(x_added, (pair + 1) * (2 * NT))
            expert_pair(PAIRS - 1, True)
            for i in range(3, 2 * NT):
                last_put(i)


_INS = ["x", "positions", "g_mix", "w_in", "conv_w", "g_conv_out", "g_attn_out", "w_out", "g_ffn", "w_router",
        "w_gate", "w_up", "w_down", "g_final"]


def kernel(**inputs):
    import concourse.bacc as bacc
    from concourse.bass_utils import run_bass_kernel_spmd

    nc = bacc.Bacc("TRN2", target_bir_lowering=False, num_devices=1)
    arrays, args = {}, []
    for name in _INS:
        a = np.ascontiguousarray(inputs[name])
        arrays[f"in_{name}"] = a
        args.append(nc.dram_tensor(f"in_{name}", a.shape, mybir.dt.from_np(a.dtype), kind="ExternalInput").ap())
    out = nc.dram_tensor("out_0", inputs["x"].shape, F32, kind="ExternalOutput").ap()
    hybrid_layer(nc, *args, out)
    r = run_bass_kernel_spmd(nc, [arrays], core_ids=[0])
    return r.results[0]["out_0"]
```
